# Optimizing a Trainium2 kernel written in Bass

```python
import math
import jax, jax.numpy as jnp
from jax import lax
import numpy as np

D_MODEL = 1024
BATCH = 1
SEQ = 1024
DEPTH = 1
DEC_BATCH = 8
DEC_SEQ = 16
PAST_LEN = 2048

CHUNK = 64
Q_BLOCK = 128
HEAD_DIM = 64
N_HEADS_A = 8
N_HEADS_B = 8
WIDTH_A = N_HEADS_A * HEAD_DIM
WIDTH_B = N_HEADS_B * HEAD_DIM
MIX_WIDTH = WIDTH_A + WIDTH_B
IN_DIM = 4 * WIDTH_A + N_HEADS_A + 4 * WIDTH_B
EPS = 1e-6
FORGET_BIAS_INIT = 3.0

kernel_name = "fox_stickbreak_hybrid_stream_step"

def rmsnorm(x, g):
    xf = x.astype(jnp.float32)
    y = xf * lax.rsqrt(jnp.mean(xf * xf, axis=-1, keepdims=True) + EPS)
    return (y * g.astype(jnp.float32)).astype(x.dtype)

def project(h, w_in, b_f):
    b, t, _ = h.shape
    u = jnp.einsum("btd,de->bte", h, w_in)
    sizes = (WIDTH_A, WIDTH_A, WIDTH_A, N_HEADS_A, WIDTH_A,
             WIDTH_B, WIDTH_B, WIDTH_B, WIDTH_B)
    idx, acc = [], 0
    for s in sizes[:-1]:
        acc += s
        idx.append(acc)
    qa, ka, va, fa, za, qb, kb, vb, zb = jnp.split(u, idx, axis=-1)
    hd = lambda a, n: a.reshape(b, t, n, HEAD_DIM)
    logf = jax.nn.log_sigmoid((fa + b_f).astype(jnp.float32))
    return (hd(qa, N_HEADS_A), hd(ka, N_HEADS_A), hd(va, N_HEADS_A), logf, za,
            hd(qb, N_HEADS_B), hd(kb, N_HEADS_B), hd(vb, N_HEADS_B), zb)

def fox_attend(q, k, v, cq, ck, q_pos, k_pos):
    s = jnp.einsum("bqhd,bkhd->bhqk", q, k, preferred_element_type=jnp.float32) * (HEAD_DIM ** -0.5)
    bias = jnp.swapaxes(cq, 1, 2)[:, :, :, None] - jnp.swapaxes(ck, 1, 2)[:, :, None, :]
    mask = k_pos[None, :] <= q_pos[:, None]
    p = jax.nn.softmax(jnp.where(mask, s + bias, -jnp.inf), axis=-1)
    return jnp.einsum("bhqk,bkhd->bqhd", p.astype(v.dtype), v)

def sb_attend(q, k, v, q_pos, k_pos):
    z = jnp.einsum("bqhd,bkhd->bhqk", q, k, preferred_element_type=jnp.float32) * (HEAD_DIM ** -0.5)
    mask = k_pos[None, :] < q_pos[:, None]
    log_1m = jnp.where(mask, jax.nn.log_sigmoid(-z), 0.0)
    suffix = lax.cumsum(log_1m, axis=3, reverse=True) - log_1m
    a = jnp.where(mask, jnp.exp(jax.nn.log_sigmoid(z) + suffix), 0.0)
    return jnp.einsum("bhqk,bkhd->bqhd", a.astype(v.dtype), v)

def merge(oa, za, ob, zb, gn_a, gn_b, w_out):
    b, t = oa.shape[0], oa.shape[1]
    ya = rmsnorm(oa.reshape(b, t, WIDTH_A), gn_a) * jax.nn.silu(za)
    yb = rmsnorm(ob.reshape(b, t, WIDTH_B), gn_b) * jax.nn.silu(zb)
    return jnp.einsum("bte,ed->btd", jnp.concatenate([ya, yb], axis=-1), w_out)

def prompt_attention(qa, ka, va, logf, qb, kb, vb):
    t = qa.shape[1]
    c = jnp.cumsum(logf, axis=1)
    pos = jnp.arange(t)
    outs_a, outs_b = [], []
    for i in range(t // Q_BLOCK):
        lo, hi = i * Q_BLOCK, (i + 1) * Q_BLOCK
        outs_a.append(fox_attend(qa[:, lo:hi], ka[:, :hi], va[:, :hi],
                                 c[:, lo:hi], c[:, :hi], pos[lo:hi], pos[:hi]))
        outs_b.append(sb_attend(qb[:, lo:hi], kb[:, :hi], vb[:, :hi], pos[lo:hi], pos[:hi]))
    return jnp.concatenate(outs_a, axis=1), jnp.concatenate(outs_b, axis=1)

def sample_attention(qa, ka, va, logf, qb, kb, vb, ck_a, cv_a, cf_a, ck_b, cv_b):
    p, t = ck_a.shape[1], qa.shape[1]
    ka_all = jnp.concatenate([ck_a.astype(ka.dtype), ka], axis=1)
    va_all = jnp.concatenate([cv_a.astype(va.dtype), va], axis=1)
    kb_all = jnp.concatenate([ck_b.astype(kb.dtype), kb], axis=1)
    vb_all = jnp.concatenate([cv_b.astype(vb.dtype), vb], axis=1)
    c_all = jnp.cumsum(jnp.concatenate([cf_a.astype(jnp.float32), logf], axis=1), axis=1)
    k_pos = jnp.arange(p + t)
    q_pos = p + jnp.arange(t)
    oa = fox_attend(qa, ka_all, va_all, c_all[:, p:], c_all, q_pos, k_pos)
    ob = sb_attend(qb, kb_all, vb_all, q_pos, k_pos)
    return oa, ob

def setup_inputs(seed: int = 0) -> dict:
    key = jax.random.key(seed)
    ks = jax.random.split(key, 16)
    nrm = lambda k, shape: jax.random.normal(k, shape, jnp.float32)
    cache_a = (DEPTH, DEC_BATCH, PAST_LEN, N_HEADS_A, HEAD_DIM)
    cache_b = (DEPTH, DEC_BATCH, PAST_LEN, N_HEADS_B, HEAD_DIM)
    return {
        "x_prompt": nrm(ks[0], (BATCH, SEQ, D_MODEL)),
        "x_sample": nrm(ks[1], (DEC_BATCH, DEC_SEQ, D_MODEL)),
        "cache_fox_k": nrm(ks[2], cache_a),
        "cache_fox_v": nrm(ks[3], cache_a),
        "cache_fox_logf": jax.nn.log_sigmoid(FORGET_BIAS_INIT + nrm(ks[4], (DEPTH, DEC_BATCH, PAST_LEN, N_HEADS_A))),
        "cache_sb_k": nrm(ks[5], cache_b),
        "cache_sb_v": nrm(ks[6], cache_b),
        "norm_g": 1.0 + 0.01 * nrm(ks[7], (DEPTH, D_MODEL)),
        "w_in": nrm(ks[8], (DEPTH, D_MODEL, IN_DIM)) * D_MODEL ** -0.5,
        "b_f": FORGET_BIAS_INIT + 0.1 * nrm(ks[9], (DEPTH, N_HEADS_A)),
        "out_norm_a": 1.0 + 0.01 * nrm(ks[10], (DEPTH, WIDTH_A)),
        "out_norm_b": 1.0 + 0.01 * nrm(ks[11], (DEPTH, WIDTH_B)),
        "w_out": nrm(ks[12], (DEPTH, MIX_WIDTH, D_MODEL)) * MIX_WIDTH ** -0.5,
        "final_norm_g": 1.0 + 0.01 * nrm(ks[13], (D_MODEL,)),
    }

def reference(x_prompt, x_sample, cache_fox_k, cache_fox_v, cache_fox_logf, cache_sb_k, cache_sb_v,
              norm_g, w_in, b_f, out_norm_a, out_norm_b, w_out, final_norm_g):
    xp, xs = x_prompt, x_sample
    p_ka, p_va, p_fa, p_kb, p_vb = [], [], [], [], []
    s_ka, s_va, s_fa, s_kb, s_vb = [], [], [], [], []
    for l in range(DEPTH):
        hp = rmsnorm(xp, norm_g[l])
        qa, ka, va, logf, za, qb, kb, vb, zb = project(hp, w_in[l], b_f[l])
        oa, ob = prompt_attention(qa, ka, va, logf, qb, kb, vb)
        xp = xp + merge(oa, za, ob, zb, out_norm_a[l], out_norm_b[l], w_out[l])
        p_ka.append(ka); p_va.append(va); p_fa.append(logf); p_kb.append(kb); p_vb.append(vb)

        hs = rmsnorm(xs, norm_g[l])
        qa, ka, va, logf, za, qb, kb, vb, zb = project(hs, w_in[l], b_f[l])
        oa, ob = sample_attention(qa, ka, va, logf, qb, kb, vb,
                                  cache_fox_k[l], cache_fox_v[l], cache_fox_logf[l],
                                  cache_sb_k[l], cache_sb_v[l])
        xs = xs + merge(oa, za, ob, zb, out_norm_a[l], out_norm_b[l], w_out[l])
        s_ka.append(ka); s_va.append(va); s_fa.append(logf); s_kb.append(kb); s_vb.append(vb)

    y_prompt = rmsnorm(xp, final_norm_g)
    y_sample = rmsnorm(xs, final_norm_g)
    return (y_prompt, y_sample,
            jnp.stack(p_ka), jnp.stack(p_va), jnp.stack(p_fa), jnp.stack(p_kb), jnp.stack(p_vb),
            jnp.stack(s_ka), jnp.stack(s_va), jnp.stack(s_fa), jnp.stack(s_kb), jnp.stack(s_vb))


_drawn_inputs = setup_inputs


def setup_inputs(seed=0):
    import zlib

    import numpy as np

    out = dict(_drawn_inputs(seed))
    spreads = {}
    factors = {'norm_g': 5.707,
     'out_norm_a': 61.212,
     'out_norm_b': 61.87,
     'final_norm_g': 29.968,
     'cache_fox_logf': 5.071}
    for name, (base, spread) in spreads.items():
        noise = np.random.default_rng([zlib.crc32(name.encode()), seed]).standard_normal(out[name].shape)
        drawn = base * np.exp(spread * noise) if base else spread * noise
        out[name] = __import__('jax').numpy.asarray(drawn.astype(out[name].dtype))
    for name, factor in factors.items():
        out[name] = (out[name] * factor).astype(out[name].dtype)
    return out
```

```python
from contextlib import ExitStack

import concourse.bass as bass
from concourse import mybir

F32 = mybir.dt.float32
F32R = mybir.dt.float32r
BF16 = mybir.dt.bfloat16
ALU = mybir.AluOpType
ACT = mybir.ActivationFunctionType
AX = mybir.AxisListType

P = 128
EPS = 1e-6
MASKED = -(2.0 ** 100)
LOWEST = -3.0e38


def build(nc, x_prompt, x_sample, cache_fox_k, cache_fox_v, cache_fox_logf, cache_sb_k, cache_sb_v,
          norm_g, w_in, b_f, out_norm_a, out_norm_b, w_out, final_norm_g,
          y_prompt, y_sample, fk_p, fv_p, ff_p, sk_p, sv_p, fk_s, fv_s, ff_s, sk_s, sv_s, stages=4):
    _, SEQ, D = x_prompt.shape
    _, DB, PAST, H, HD = cache_fox_k.shape
    DS = x_sample.shape[1]
    KD = D // P
    TP = SEQ // P
    T = TP + 1
    TOK = T * P
    W = H * HD
    NPAIR = H // 2
    IN = w_in.shape[2]
    SCALE = HD ** -0.5
    KEYS = PAST + DS
    CH = PAST // 512
    assert (DB * DS, W, KD, TP, CH, H) == (P, 512, 8, 8, 4, 8)
    BLOCK_AT = [0, W, 2 * W, 3 * W + H, 4 * W + H, 5 * W + H, 6 * W + H, 7 * W + H]
    F_AT = 3 * W
    NB = len(BLOCK_AT)

    q_d = nc.dram_tensor("q_scratch", (TOK, 2 * W), F32).ap()
    z_d = nc.dram_tensor("z_scratch", (TOK, 2 * W), F32).ap()
    c_d = nc.dram_tensor("c_scratch", (H, SEQ), F32).ap()

    xp_v = x_prompt[0].rearrange("(t p) d -> t p d", p=P)
    xs_v = x_sample.rearrange("b s d -> (b s) d")
    w_v = w_in[0].rearrange("(k p) e -> p k e", p=P)
    wo_v = w_out[0].rearrange("(k p) e -> p k e", p=P)
    yp_v = y_prompt[0].rearrange("(t p) d -> t p d", p=P)
    ys_v = y_sample.rearrange("b s d -> (b s) d")

    def rows(ap):
        return ap[0].rearrange("b s h d -> (b s) (h d)")

    fkp, fvp, skp, svp = rows(fk_p), rows(fv_p), rows(sk_p), rows(sv_p)
    fks, fvs, sks, svs = rows(fk_s), rows(fv_s), rows(sk_s), rows(sv_s)
    def block_rows(c, rows, sample):
        kind, g = c % 4, c // 4
        if kind in (0, 3):
            return (z_d if kind else q_d)[rows, g * W:g * W + W]
        at = [[[fkp, fks], [skp, sks]], [[fvp, fvs], [svp, svs]]][kind - 1][g][sample]
        return at if sample else at[rows]

    sems = ExitStack()

    def sem(name):
        return sems.enter_context(nc.semaphore(name))

    def allocator(stack, kind):
        make = nc.sbuf_tensor if kind == "sbuf" else nc.psum_tensor
        return lambda name, shape, dt: stack.enter_context(make(name, shape, dt))

    with sems, ExitStack() as keep:
        sb = allocator(keep, "sbuf")
        ident = sb("ident", [P, P], F32)
        identb = sb("identb", [P, P], BF16)
        mask = [sb("mask_fox", [P, P], BF16), sb("mask_sb", [P, P], BF16)]
        tselb = sb("tselb", [DS, P], BF16)
        pickf = sb("pickf", [P, DB, P], F32)
        neghalf = sb("neghalf", [P, 2], F32)
        zero = sb("zero", [P, 1], F32)
        qs = sb("qs", [P, 2, DB, NPAIR, 2 * DS], F32)
        kns = sb("kns", [P, 2, NPAIR, P], F32)
        stat = sb("stat", [P, 64], F32)
        rowmax = sb("rowmax", [P, 4], F32)
        negmax = sb("negmax", [P, 4], F32)
        rowsum = sb("rowsum", [P, TP, 2], F32)
        rowinv = sb("rowinv", [P, TP, 2], F32)
        d_max = sb("d_max", [P, CH + 2], F32)
        d_neg = sb("d_neg", [P, 1], F32)
        d_sum = sb("d_sum", [P, 1], F32)
        d_inv = sb("d_inv", [P, 1], F32)
        m_stat = sb("m_stat", [P, 3, T, 4], F32)

        one = ExitStack()
        sb1 = allocator(one, "sbuf")
        hT_hi = sb1("hT_hi", [P, KD, TOK], F32R)
        hT_lo = sb1("hT_lo", [P, KD, TOK], F32R)
        w_raw = sb1("w_raw", [P, 2, KD // 2, W], F32)
        w_hi = sb1("w_hi", [P, 2, KD, W], F32R)
        w_lo = sb1("w_lo", [P, 2, KD, W], F32R)
        u_out = sb1("u_out", [P, 3, W], F32)
        x_in = sb1("x_in", [P, 2, D], F32)
        h_nat = sb1("h_nat", [P, D], F32)
        ng_b = sb1("ng_b", [P, D], F32)
        wf_raw = sb1("wf_raw", [P, KD, H], F32)
        wf_hi = sb1("wf_hi", [P, KD, H], F32R)
        wf_lo = sb1("wf_lo", [P, KD, H], F32R)
        bf_col = sb1("bf_col", [H, 1], F32)
        fx = sb1("fx", [H, TOK], F32)
        fe = sb1("fe", [H, TOK], F32)
        lfT = fe
        c8 = fx[:, 0:SEQ]
        lf_nat = sb1("lf_nat", [P, T, H], F32)
        one.close()

        sb_o = allocator(keep, "sbuf")
        o_nat = sb_o("o_nat", [P, T, D], F32)
        k_ring = sb_o("k_ring", [P, CH, 4, W], F32)
        late = ExitStack()
        sb_l = allocator(late, "sbuf")
        v_ring = sb_l("v_ring", [P, CH, 4, W], F32)
        c_b = k_ring[:, 0, :, :].rearrange("p a c -> p (a c)").rearrange("p (h s) -> p h s", h=2)
        scratch = v_ring[:, :, :, :].rearrange("p a b c -> p (a b c)")
        q_sn = scratch[:, 0:2 * W]
        k_sn = scratch[:, 2 * W:4 * W]
        l_in = o_nat[:, 0, :]
        l_nat = scratch[:, 4 * W:6 * W].rearrange("p (j m) -> p j m", j=4 * CH)
        cT = scratch[0:DB * H, 6 * W:6 * W + KEYS]
        cT8 = scratch[0:DB * H, 11 * W:11 * W + KEYS]

        two = ExitStack()
        sb2 = allocator(two, "sbuf")
        q_nat = sb2("q_nat", [P, TP, 2, P], F32)
        k_nat = sb2("k_nat", [P, TP, 2, P], F32)
        v_nat = sb2("v_nat", [P, TP, P], F32)
        q_hh = sb2("q_hh", [P, 2, SEQ], F32R)
        q_ll = sb2("q_ll", [P, 2, SEQ], F32R)
        k_hl = sb2("k_hl", [P, 2, SEQ], F32R)
        pr = sb2("pr", [P, 4, SEQ], F32)
        om = sb2("om", [P, 4, SEQ], F32)
        pT = sb2("pT", [P, 4, 512], F32)
        oT = sb2("oT", [P, 512], F32)
        two.close()

        three = ExitStack()
        sb3 = allocator(three, "sbuf")
        kT = sb3("kT", [P, 2, NPAIR, 512], F32)
        d_s = sb3("d_s", [P, KEYS], F32)
        d_om = sb3("d_om", [P, KEYS], F32)
        d_p = sb3("d_p", [P, KEYS], F32)
        d_pT = sb3("d_pT", [P, 4 * CH, P], F32)
        d_pTn = sb3("d_pTn", [DS, P], F32)
        v_new = sb3("v_new", [DS, W], F32)
        q_cur = sb3("q_cur", [P, NPAIR, 2 * DS], F32)
        kn_cur = sb3("kn_cur", [P, NPAIR, DS], F32)
        pick_cur = sb3("pick_cur", [P, P], F32R)
        c_hl = sb3("c_hl", [P, KEYS], F32R)
        o_d = sb3("o_d", [P, P], F32)
        oT_s = sb3("oT_s", [P, 2, NPAIR, P], F32)
        three.close()
        late.close()

        four = ExitStack()
        sb4 = allocator(four, "sbuf")
        wo_lo = sb4("wo_lo", [P, KD, D], F32R)
        wo_hi = sb4("wo_hi", [P, KD, D], F32R)
        zt = sb4("zt", [P, 2, D], F32)
        xt = sb4("xt", [P, 2, D], F32)
        sg = sb4("sg", [P, D], F32)
        yg = sb4("yg", [P, D], F32)
        yT_hi = sb4("yT_hi", [P, 2, KD, P], F32R)
        yT_lo = sb4("yT_lo", [P, 2, KD, P], F32R)
        gn_b = sb4("gn_b", [P, D], F32)
        fg_b = sb4("fg_b", [P, D], F32)
        junk = sb4("junk", [P, D], F32)
        four.close()

        bank = allocator(keep, "psum")("bank", [P, 8, 512], F32)
        U, TR = 0, 4
        SC, PTB, PV, MI = 0, 4, 6, 7
        DSC, DNEW, MIX = 4, 6, 7

        def flat(ap):
            return ap.rearrange("p a b -> p (a b)")

        consts = sem("consts")
        pool_step = sem("pool_step")
        x_loaded = [sem("x_loaded0"), sem("x_loaded1")]
        g_loaded = sem("g_loaded")
        bf_loaded = sem("bf_loaded")
        wf_loaded = sem("wf_loaded")
        w_loaded = [sem("w_loaded0"), sem("w_loaded1")]
        sq_done, ms_done, rstd_done = sem("sq_done"), sem("ms_done"), sem("rstd_done")
        h_ready, htp_ready, hhi_done, hlo_done = sem("h_ready"), sem("htp_ready"), sem("hhi_done"), sem("hlo_done")
        whi_done, wlo_done = sem("whi_done"), sem("wlo_done")
        wfhi_done, wflo_done = sem("wfhi_done"), sem("wflo_done")
        u_ready, u_moved = sem("u_ready"), sem("u_moved")
        u_stored = [sem("u_stored0"), sem("u_stored1"), sem("u_stored2")]
        f_ready, f_moved, f_act, lf_done, lft_ready, lfn_done = (
            sem("f_ready"), sem("f_moved"), sem("f_act"), sem("lf_done"), sem("lft_ready"), sem("lfn_done"))
        c8_step = sem("c8_step")
        lf_stored, c8_stored = sem("lf_stored"), sem("c8_stored")

        def plain_wait(eng, semaphore, value):
            eng.wait_ge(semaphore, value)
            eng.nop(nofuse=True)

        def x_rows(t):
            return xp_v[t] if t < TP else xs_v

        def sp_project(sp):
            def load_x(t):
                if t >= 2:
                    sp.wait_ge(h_ready, t - 1)
                sp.dma_start(x_in[:, t % 2, :], x_rows(t)).then_inc(x_loaded[t % 2], 16)

            def load_w(c, half):
                if c >= 1:
                    sp.wait_ge(wlo_done, 2 * (c - 1) + half + 1)
                sp.dma_start(w_raw[:, half], w_v[:, half * 4:half * 4 + 4, BLOCK_AT[c]:BLOCK_AT[c] + W]
                             ).then_inc(w_loaded[half], 16)

            def store(c, r, s):
                sp.wait_ge(u_moved, 9 * c + 3 * r + s + 1)
                sample = isinstance(r, int) and 3 * r + s == TP
                sp.dma_start(block_rows(c, bass.ds((3 * r + s) * P, P), sample), u_out[:, s, :]).then_inc(u_stored[s], 16)

            load_x(0)
            sp.dma_start(ng_b[:], norm_g.to_broadcast([P, D])
                         ).then_inc(g_loaded, 16)
            load_w(0, 0)
            load_x(1)
            load_w(0, 1)
            sp.dma_start(wf_raw[:], w_v[:, :, F_AT:F_AT + H]).then_inc(wf_loaded, 16)
            sp.dma_start(bf_col[:], b_f.rearrange("a h -> h a")).then_inc(bf_loaded, 16)
            for t in range(2, T):
                load_x(t)
                if t == 3:
                    load_w(1, 0)
                if t == 5:
                    load_w(1, 1)
                if t >= 4:
                    store(0, (t - 4) // 3, (t - 4) % 3)
            for t in range(T - 4, T):
                store(0, t // 3, t % 3)
            load_w(2, 0)
            load_w(2, 1)
            for c in range(1, NB):
                with sp.Fori(0, 2) as r:
                    for s in range(3):
                        store(c, r, s)
                if c < NB - 2:
                    load_w(c + 2, 0)
                for s in range(3):
                    store(c, 2, s)
                if c < NB - 2:
                    load_w(c + 2, 1)
                if c == 2:
                    sp.wait_ge(lfn_done, 1)
                    sp.dma_start(ff_p[0, 0].rearrange("(t p) h -> p t h", p=P), lf_nat[:, 0:TP, :]
                                 ).then_inc(lf_stored, 16)
                    sp.dma_start(ff_s[0].rearrange("b s h -> (b s) h"), lf_nat[:, TP, :]).then_inc(lf_stored, 16)
                    sp.wait_ge(c8_step, 2)
                    sp.dma_start(c_d, c8).then_inc(c8_stored, 16)
            for s in range(3):
                sp.wait_ge(u_stored[s], 16 * 3 * NB)
            sp.wait_ge(lf_stored, 32)
            sp.wait_ge(c8_stored, 16)

        def act_project(act):
            def w_split(c, half):
                act.wait_ge(w_loaded[half], 16 * (c + 1))
                if not isinstance(c, int) or c >= 2:
                    act.wait_ge(u_ready, 9 * (c - 1))
                act.activation(w_hi[:, split_parity[0], half * 4:half * 4 + 4, :], w_raw[:, half], ACT.Copy
                               ).then_inc(whi_done, 1)

            split_parity = [0]

            def h_square(t):
                act.wait_ge(x_loaded[t % 2], 16 * (t // 2 + 1))
                if t >= 1:
                    act.wait_ge(htp_ready, 2 * t)
                act.activation(h_nat[:], x_in[:, t % 2, :], ACT.Square, accum_out=stat[:, t:t + 1]).then_inc(sq_done, 1)

            def h_hi(t):
                for b in range(2):
                    act.wait_ge(htp_ready, 2 * t + b + 1)
                    act.activation(hT_hi[:, 4 * b:4 * b + 4, t * P:t * P + P],
                                   bank[:, TR + b, :].rearrange("p (k s) -> p k s", k=4), ACT.Copy
                                   ).then_inc(hhi_done, 1)

            def u_move(c, t):
                act.wait_ge(u_ready, 9 * c + t + 1)
                if not isinstance(c, int) or 9 * c + t >= 3:
                    act.wait_ge(u_stored[t % 3], 16 * (3 * c + t // 3))
                act.activation(u_out[:, t % 3, :], bank[:, U + t % 3, :], ACT.Copy).then_inc(u_moved, 1)

            def block(c, par, split):
                for t in range(T):
                    u_move(c, t)
                    if split and t in (1, 4):
                        split_parity[0] = 1 - par
                        w_split(c + 1, 0 if t == 1 else 1)

            h_square(0)
            h_hi(0)
            w_split(0, 0)
            h_square(1)
            w_split(0, 1)
            h_hi(1)
            for t in range(2, T):
                h_square(t)
                h_hi(t)
                if t == 2:
                    act.wait_ge(wf_loaded, 16)
                    act.activation(wf_hi[:], wf_raw[:], ACT.Copy).then_inc(wfhi_done, 1)
                u_move(0, t - 2)
            split_parity[0] = 1
            w_split(1, 0)
            w_split(1, 1)
            u_move(0, T - 2)
            u_move(0, T - 1)
            block(1, 1, True)
            act.wait_ge(bf_loaded, 16)
            for m in range(3):
                act.wait_ge(f_ready, m + 1)
                act.activation(fx[:, 384 * m:384 * m + 384], bank[0:H, TR + m % 2, 0:384], ACT.Identity,
                               bias=bf_col[:, 0:1]).then_inc(f_moved, 1)
            act.wait_ge(f_moved, 3)
            act.activation(fe[:], fx[:], ACT.Abs).then_inc(f_act, 1)
            act.wait_ge(f_act, 1)
            act.activation(fe[:], fe[:], ACT.Exp, scale=-1.0).then_inc(f_act, 1)
            act.wait_ge(f_act, 2)
            act.activation(fe[:], fe[:], ACT.Ln, bias=1.0).then_inc(f_act, 1)
            with act.Fori(1, NB // 2 - 1) as c2:
                block(2 * c2, 0, True)
                block(2 * c2 + 1, 1, True)
            block(NB - 2, 0, True)
            block(NB - 1, 1, False)

        def dve_project(dve):
            def w_lo_part(c, half, par):
                dve.wait_ge(whi_done, 2 * c + half + 1)
                dve.tensor_tensor(w_lo[:, par, half * 4:half * 4 + 4, :], w_raw[:, half],
                                  w_hi[:, par, half * 4:half * 4 + 4, :].bitcast(F32), ALU.subtract
                                  ).then_inc(wlo_done, 1)

            def h_scale(t):
                dve.wait_ge(sq_done, t + 1)
                dve.tensor_scalar(stat[:, 16 + t:17 + t], stat[:, t:t + 1], 1.0 / D, EPS, ALU.mult, ALU.add
                                  ).then_inc(ms_done, 1)
                dve.wait_ge(rstd_done, t + 1)
                dve.scalar_tensor_tensor(out=h_nat[:], in0=x_in[:, t % 2, :], scalar=stat[:, 32 + t:33 + t],
                                         in1=ng_b[:], op0=ALU.mult, op1=ALU.mult).then_inc(h_ready, 1)

            def h_lo(t):
                for b in range(2):
                    dve.wait_ge(hhi_done, 2 * t + b + 1)
                    dve.tensor_tensor(hT_lo[:, 4 * b:4 * b + 4, t * P:t * P + P],
                                      bank[:, TR + b, :].rearrange("p (k s) -> p k s", k=4),
                                      hT_hi[:, 4 * b:4 * b + 4, t * P:t * P + P].bitcast(F32), ALU.subtract
                                      ).then_inc(hlo_done, 1)

            dve.wait_ge(g_loaded, 16)
            h_scale(0)
            h_lo(0)
            w_lo_part(0, 0, 0)
            h_scale(1)
            w_lo_part(0, 1, 0)
            h_lo(1)
            for t in range(2, T):
                h_scale(t)
                h_lo(t)
                if t == 2:
                    dve.wait_ge(wfhi_done, 1)
                    dve.tensor_tensor(wf_lo[:], wf_raw[:], wf_hi[:].bitcast(F32), ALU.subtract).then_inc(wflo_done, 1)
            for c in (1, 2):
                for half in range(2):
                    w_lo_part(c, half, c % 2)
            dve.wait_ge(f_act, 3)
            dve.scalar_tensor_tensor(out=lfT[:], in0=fx[:], scalar=0.0, in1=fe[:], op0=ALU.min, op1=ALU.subtract
                                     ).then_inc(lf_done, 1)
            dve.wait_ge(lf_done, 1)
            dve.tensor_tensor_scan(c8, lfT[:, 0:SEQ], lfT[:, 0:SEQ], 0.0, ALU.add, ALU.bypass).then_inc(c8_step, 1)
            dve.wait_ge(c8_step, 1)
            dve.tensor_scalar(c8, c8, -1.0 / SCALE, None, ALU.mult).then_inc(c8_step, 1)
            dve.wait_ge(lft_ready, 1)
            dve.tensor_copy(flat(lf_nat[:]), bank[:, TR + 1, 0:T * H]).then_inc(lfn_done, 1)
            with dve.Fori(1, NB // 2 - 1) as c2:
                for half in range(2):
                    w_lo_part(2 * c2 + 1, half, 1)
                for half in range(2):
                    w_lo_part(2 * c2 + 2, half, 0)
            for half in range(2):
                w_lo_part(NB - 1, half, 1)

        def pool_project(pool):
            for t in range(T):
                pool.wait_ge(ms_done, t + 1)
                pool.tensor_tensor(stat[:, 32 + t:33 + t], stat[:, 16 + t:17 + t], neghalf[:, 0:1], ALU.pow
                                   ).then_inc(rstd_done, 1)

        def pe_project(pe):
            def h_transpose(t):
                pe.wait_ge(h_ready, t + 1)
                if t >= 1:
                    pe.wait_ge(hlo_done, 2 * t)
                for b in range(2):
                    for k in range(4):
                        mm = pe.transpose(bank[:, TR + b, k * P:k * P + P], h_nat[:, (4 * b + k) * P:(4 * b + k + 1) * P],
                                          ident[:])
                    mm.then_inc(htp_ready, 1)

            def multiply(c, t, par):
                if not isinstance(c, int) or 9 * c + t >= 3:
                    pe.wait_ge(u_moved, 9 * c + t - 2)
                for k in range(KD):
                    for n, (a, b) in enumerate(((hT_hi, w_hi), (hT_hi, w_lo), (hT_lo, w_hi))):
                        mm = pe.matmul(bank[:, U + t % 3, :], a[:, k, t * P:t * P + P], b[:, par, k, :],
                                       start=(k == 0 and n == 0), stop=(k == KD - 1 and n == 2))
                mm.then_inc(u_ready, 1)

            def block(c, par):
                pe.wait_ge(wlo_done, 2 * (c + 1))
                for t in range(T):
                    multiply(c, t, par)

            pe.wait_ge(consts, 1)
            h_transpose(0)
            for t in range(T):
                if t < T - 1:
                    h_transpose(t + 1)
                pe.wait_ge(hlo_done, 2 * (t + 1))
                if t == 0:
                    pe.wait_ge(wlo_done, 2)
                multiply(0, t, 0)
            block(1, 1)
            pe.wait_ge(wflo_done, 1)
            for m in range(3):
                if m == 2:
                    pe.wait_ge(f_moved, 1)
                for k in range(KD):
                    for n, (a, b) in enumerate(((wf_hi, hT_hi), (wf_lo, hT_hi), (wf_hi, hT_lo))):
                        mm = pe.matmul(bank[0:H, TR + m % 2, 0:384], a[:, k, :], b[:, k, 384 * m:384 * m + 384],
                                       start=(k == 0 and n == 0), stop=(k == KD - 1 and n == 2))
                mm.then_inc(f_ready, 1)
            block(2, 0)
            pe.wait_ge(lf_done, 1)
            for t in range(T):
                mm = pe.transpose(bank[:, TR + 1, t * H:t * H + H], lfT[:, t * P:t * P + P], ident[0:H, 0:H])
            mm.then_inc(lft_ready, 1)
            block(3, 1)
            with pe.Fori(2, NB // 2) as c2:
                block(2 * c2, 0)
                block(2 * c2 + 1, 1)


        AHEAD = 2
        PREP = [("k", 0), ("k", 1), ("q", 1), ("q", 0)]
        PREP_AT = {0: 0, 1: 1, 3: 2, 4: 3}
        TURN_LAST_AT, MOVE_LAST_AT, TURN_AT, MOVE_AT = 2, 1, 6, 5
        NU = TP
        NHEAD = 2 * 2 * NPAIR
        TRB = [(TP - u + 3) // 4 for u in range(NU)]
        TRA = [sum(TRB[:u]) for u in range(NU + 1)]
        NTR = TRA[NU]
        sn_loaded, lc_loaded, ln_loaded = sem("sn_loaded"), sem("lc_loaded"), sem("ln_loaded")
        cb_loaded = [sem("cb_loaded0"), sem("cb_loaded1")]
        q_loaded = [sem("q_loaded0"), sem("q_loaded1")]
        k_loaded = [sem("k_loaded0"), sem("k_loaded1")]
        v_loaded = [sem("v_loaded0"), sem("v_loaded1")]
        lc_sorted = sem("lc_sorted")
        qs_zero, sn_ready, sn_moved = sem("qs_zero"), sem("sn_ready"), sem("sn_moved")
        lc_ready, lc_moved, ct_step = sem("lc_ready"), sem("lc_moved"), sem("ct_step")
        prep_tp, prep_hi, prep_done = sem("prep_tp"), sem("prep_hi"), sem("prep_done")
        sc_ready, s_moved = sem("sc_ready"), sem("s_moved")
        negmax_ready, pf_ready = sem("negmax_ready"), sem("pf_ready")
        sig_step, scan_done, pb_ready = sem("sig_step"), sem("scan_done"), sem("pb_ready")
        pt_ready, pt_moved_act, pt_moved_dve = sem("pt_ready"), sem("pt_moved_act"), sem("pt_moved_dve")
        pv_done, ot_moved, otr_ready, rinv_done, on_done = (
            sem("pv_done"), sem("ot_moved"), sem("otr_ready"), sem("rinv_done"), sem("on_done"))

        def later(n, least):
            return not isinstance(n, int) or n >= least

        def head_of(p, hh):
            return 2 * p + hh

        def unit_of(p, hh, u):
            return 16 * p + 8 * hh + u

        def ahead_of(p, hh, u):
            v = u + AHEAD
            if v < NU:
                return p, hh, v
            return (p, 1, v - NU) if hh == 0 else (p + 1, 0, v - NU)

        def run_pairs(eng, start, pair):
            start()
            pair(0, 0, 0)
            with eng.Fori(1, NPAIR - 1) as p:
                pair(p, 0, 0)
            pair(NPAIR - 1, 0, 1)
            pair(NPAIR, 1, 1)
            with eng.Fori(NPAIR + 1, 2 * NPAIR - 1) as p:
                pair(p, 1, 1)
            pair(2 * NPAIR - 1, 1, None)

        def steps(p, g, g_next):
            for hh in range(2):
                for u in range(NU):
                    ahead = ahead_of(p, hh, u)
                    g_ahead = g_next if hh == 1 and u + AHEAD >= NU else g
                    if g_ahead is None:
                        ahead = None
                    following = (p, 1) if hh == 0 else (p + 1, 0)
                    if hh == 1 and g_next is None:
                        following = None
                    yield hh, u, ahead, g_ahead, following

        def sc_view(u, n):
            return flat(bank[:, SC + 2 * (u % 2):SC + 2 * (u % 2) + 2, :])[:, 0:n]

        def sp_prompt(sp):
            sp.dma_start(q_sn, q_d[SEQ:TOK, :]).then_inc(sn_loaded, 16)
            sp.dma_start(k_sn[:, 0:W], fks).then_inc(sn_loaded, 16)
            sp.dma_start(k_sn[:, W:], sks).then_inc(sn_loaded, 16)
            sp.dma_start(l_in.rearrange("p (b m) -> p b m", b=DB),
                         cache_fox_logf[0].rearrange("b (p j) h -> p b (j h)", p=P)).then_inc(lc_loaded, 16)

            def load_twice(dst, src, col, hh, s):
                rows_of = src[0:SEQ, bass.ds(col + hh * HD, HD)].rearrange("(t p) d -> p t d", p=P)
                for half in range(2):
                    sp.dma_start(dst[:, :, hh, half * HD:half * HD + HD], rows_of).then_inc(s[hh], 16)

            def load_qk(p, hh, g):
                load_twice(k_nat, skp if g else fkp, (p - NPAIR * g) * P, hh, k_loaded)
                load_twice(q_nat, q_d, p * P, hh, q_loaded)

            def load_v(p, hh, g):
                src = (svp if g else fvp)[:, bass.ds((p - NPAIR * g) * P + hh * HD, HD)]
                sp.dma_start(v_nat[:, :, hh * HD:hh * HD + HD], src.rearrange("(t p) e -> p t e", p=P)
                             ).then_inc(v_loaded[hh], 16)

            def load_c(p, hh):
                sp.dma_start(c_b[:, hh, :], c_d[bass.ds(head_of(p, hh), 1)].to_broadcast([P, SEQ])
                             ).then_inc(cb_loaded[hh], 16)

            for hh in range(2):
                load_qk(0, hh, 0)
                load_c(0, hh)
                load_v(0, hh, 0)
            with nc.allow_non_contiguous_dma(reason="1024 values in all"):
                for b in range(DB):
                    sp.dma_start(cT[b * H:b * H + H, PAST:KEYS], ff_s[0, b].rearrange("s h -> h s")
                                 ).then_inc(ln_loaded, 16)

            def next_pair(p, g):
                for hh in range(2):
                    sp.wait_ge(prep_tp, 4 * head_of(p, hh) + 4)
                    load_qk(p + 1, hh, g)
                for hh in range(2):
                    if not g:
                        sp.wait_ge(s_moved, unit_of(p, hh, NU))
                        load_c(p + 1, hh)
                    sp.wait_ge(pv_done, unit_of(p, hh, NU))
                    load_v(p + 1, hh, g)

            with sp.Fori(0, NPAIR - 1) as p:
                next_pair(p, 0)
            next_pair(NPAIR - 1, 1)
            if stages >= 3:
                sp.wait_ge(s_moved, unit_of(NPAIR, 0, 0))
                for c in range(CH):
                    load_k(sp, 0, 0, 0, c)
            with sp.Fori(NPAIR, 2 * NPAIR - 1) as p:
                next_pair(p, 1)

        def pe_prompt(pe):
            pe.wait_ge(sn_loaded, 48)
            pe.wait_ge(lfn_done, 1)
            for g in range(2):
                for src, at in ((q_sn, 4), (k_sn, 6)):
                    for j in range(NPAIR):
                        mm = pe.transpose(bank[:, at + g, j * P:j * P + P], src[:, g * W + j * P:g * W + j * P + P], ident[:])
                    mm.then_inc(sn_ready, 1)
            pe.wait_ge(lc_sorted, 1)
            pe.wait_ge(u_moved, 9 * NB)
            for c in range(4):
                for j in range(4):
                    mm = pe.transpose(bank[0:DB * H, c, j * P:j * P + P], l_nat[:, 4 * c + j, :], ident[:])
                mm.then_inc(lc_ready, 1)

            def prep(p, hh, m):
                h, (kind, seg) = head_of(p, hh), PREP[m]
                if m == 0:
                    pe.wait_ge(k_loaded[hh], 32 * (p + 1))
                if m == 2:
                    pe.wait_ge(q_loaded[hh], 32 * (p + 1))
                if m:
                    pe.wait_ge(prep_done, 4 * h + m)
                elif later(h, 2):
                    pe.wait_ge(on_done, 2 * (h - 1) - 1)
                elif h == 1:
                    pe.wait_ge(prep_done, 4)
                else:
                    pe.wait_ge(sn_moved, 4)
                if m == 2 and later(h, 2):
                    pe.wait_ge(on_done, 2 * (h - 1))
                src = k_nat if kind == "k" else q_nat
                for t in range(4):
                    mm = pe.transpose(bank[:, MI, t * P:t * P + P], src[:, 4 * seg + t, hh, :], ident[:])
                mm.then_inc(prep_tp, 1)

            def scores(p, hh, u, g):
                k, i = unit_of(p, hh, u), TP - 1 - u
                n = (i + 1) * P
                if u == 0:
                    pe.wait_ge(prep_done, 4 * head_of(p, hh) + 4)
                if later(k, 2):
                    pe.wait_ge(s_moved, k - 1)
                else:
                    pe.wait_ge(lc_moved, 4)
                for seg in range((n + 511) // 512):
                    w = min(512, n - seg * 512)
                    out = bank[:, SC + 2 * (u % 2) + seg, 0:w]
                    diagonal = seg == i // 4
                    for a in (q_hh, q_ll):
                        mm = pe.matmul(out, a[:, hh, i * P:i * P + P], k_hl[:, hh, seg * 512:seg * 512 + w],
                                       start=(a is q_hh), stop=(a is q_ll and not diagonal), skip_group_check=True)
                    if diagonal:
                        mm = pe.matmul(out[:, w - P:w], identb[:], mask[g][:], start=False, stop=True,
                                       skip_group_check=True)
                mm.then_inc(sc_ready, 1)

            def transpose_p(p, hh, u, g):
                k, h, i = unit_of(p, hh, u), head_of(p, hh), TP - 1 - u
                pe.wait_ge(pb_ready if g else pf_ready, k + 1 - 64 * g)
                for n in range(TRB[u]):
                    lr = TRA[u] + n
                    if g:
                        if lr == 0:
                            pe.wait_ge(pt_moved_act, NTR // 2 * 8)
                        pe.wait_ge(pt_moved_dve, NTR // 2 * 8 + NTR * (h - 8) + lr - 1)
                    elif later(h, 1) or lr >= 2:
                        pe.wait_ge(pt_moved_dve if lr % 2 else pt_moved_act, NTR // 2 * h + lr // 2)
                    else:
                        pe.wait_ge(sn_moved, 4)
                    for j in range(4 * n, min(4 * n + 4, i + 1)):
                        mm = pe.transpose(bank[:, PTB + lr % 2, (j % 4) * P:(j % 4) * P + P],
                                          pr[:, u % 4, j * P:j * P + P], ident[:])
                    mm.then_inc(pt_ready, 1)

            def outputs(p, hh, u, g):
                h, i, half = head_of(p, hh), TP - 1 - u, u // 4
                if u == 0:
                    pe.wait_ge(v_loaded[hh], 16 * (p + 1))
                if u % 4 == 0:
                    if later(h, 1):
                        pe.wait_ge(ot_moved, 2 * h - 1 + half)
                    else:
                        pe.wait_ge(sn_moved, 4)
                for j in range(i + 1):
                    lr = TRA[u] + j // 4
                    if j % 4 == 0:
                        if g:
                            pe.wait_ge(pt_moved_dve, NTR // 2 * 8 + NTR * (h - 8) + lr + 1)
                        else:
                            pe.wait_ge(pt_moved_dve if lr % 2 else pt_moved_act, NTR // 2 * h + lr // 2 + 1)
                    mm = pe.matmul(bank[half * HD:half * HD + HD, PV, (i % 4) * P:(i % 4) * P + P],
                                   v_nat[:, j, hh * HD:hh * HD + HD], pT[:, lr % 4, (j % 4) * P:(j % 4) * P + P],
                                   start=(j == 0), stop=(j == i), skip_group_check=True)
                mm.then_inc(pv_done, 1)

            def turn(h, half, last=False):
                pe.wait_ge(ot_moved, 2 * h + half + 1)
                if not last:
                    plain_wait(pe, prep_done, 4 * (h + 2) if half == 0 else 4 * (h + 2) + 2)
                else:
                    plain_wait(pe, on_done, 2 * h + half)
                part = slice(half * HD, half * HD + HD)
                for t in range(4):
                    mm = pe.transpose(bank[:, MI, t * HD:t * HD + HD], oT[part, t * P:t * P + P], ident[part, part])
                mm.then_inc(otr_ready, 1)

            def pair(p, g, g_next):
                for hh, u, ahead, g_ahead, following in steps(p, g, g_next):
                    h = head_of(p, hh)
                    if ahead:
                        scores(*ahead, g_ahead)
                    transpose_p(p, hh, u, g)
                    if u:
                        outputs(p, hh, u - 1, g)
                    elif hh:
                        outputs(p, 0, NU - 1, g)
                    elif later(p, 1):
                        outputs(p - 1, 1, NU - 1, int(g and not (isinstance(p, int) and p == NPAIR)))
                    if u == TURN_LAST_AT and later(h, 1):
                        turn(h - 1, 1, last=following is None)
                    if u == TURN_AT:
                        turn(h, 0, last=following is None)
                    if u in PREP_AT and following:
                        prep(*following, PREP_AT[u])

            def start():
                for m in range(4):
                    prep(0, 0, m)
                for u in range(AHEAD):
                    scores(0, 0, u, 0)

            run_pairs(pe, start, pair)
            outputs(2 * NPAIR - 1, 1, NU - 1, 1)
            turn(NHEAD - 1, 1, last=True)

        def wait_unit_free(eng, p, hh, u):
            h = head_of(p, hh)
            if u >= 4:
                eng.wait_ge(pt_ready, NTR * h + TRA[u - 3])
            elif later(h, 1):
                eng.wait_ge(pt_ready, NTR * (h - 1) + TRA[u + 5])

        def move_pt(eng, p, hh, u, n):
            k, i = unit_of(p, hh, u), TP - 1 - u
            lr = TRA[u] + n
            w = min(4, i + 1 - 4 * n) * P
            eng.wait_ge(pt_ready, NTR * head_of(p, hh) + lr + 1)
            if later(k, 2):
                eng.wait_ge(pv_done, k - 1)
            return pT[:, lr % 4, 0:w], bank[:, PTB + lr % 2, 0:w]

        def act_prompt(act):
            def prep(p, hh, m):
                h, (kind, seg) = head_of(p, hh), PREP[m]
                act.wait_ge(prep_tp, 4 * h + m + 1)
                if m == 0 and later(h, 2):
                    act.wait_ge(sc_ready, NU * (h - 1))
                dst = k_hl if kind == "k" else q_hh
                act.activation(dst[:, hh, 512 * seg:512 * seg + 512], bank[:, MI, :], ACT.Copy).then_inc(prep_hi, 1)

            def softmax(p, hh, u):
                k, h, n = unit_of(p, hh, u), head_of(p, hh), (TP - u) * P
                if u % 4 == 0 and later(h, 2):
                    act.wait_ge(rinv_done, 2 * (h - 2) + u // 4 + 1)
                act.wait_ge(negmax_ready, k + 1)
                x = pr[:, u % 4, 0:n]
                act.activation(x, x, ACT.Exp, bias=negmax[:, u % 4:u % 4 + 1], scale=SCALE,
                               accum_out=rowsum[:, TP - 1 - u, hh:hh + 1]).then_inc(pf_ready, 1)

            def sigmoids(p, hh, u):
                k, n = unit_of(p, hh, u), (TP - u) * P
                wait_unit_free(act, p, hh, u)
                act.wait_ge(sc_ready, k + 1)
                act.activation(om[:, u % 4, 0:n], sc_view(u, n), ACT.Sigmoid, scale=-SCALE).then_inc(sig_step, 1)
                act.activation(pr[:, u % 4, 0:n], sc_view(u, n), ACT.Sigmoid, scale=SCALE).then_inc(s_moved, 1)

            def move_o(h, half):
                act.wait_ge(pv_done, NU * h + 4 * half + 4)
                if later(h, 1):
                    act.wait_ge(otr_ready, 2 * h - 1 + half)
                part = slice(half * HD, half * HD + HD)
                act.activation(oT[part], bank[part, PV, :], ACT.Copy).then_inc(ot_moved, 1)

            def pair(p, g, g_next):
                for hh, u, ahead, g_ahead, following in steps(p, g, g_next):
                    h = head_of(p, hh)
                    if not g:
                        for n in range(TRB[u]):
                            if (TRA[u] + n) % 2 == 0:
                                act.activation(*move_pt(act, p, hh, u, n), ACT.Copy).then_inc(pt_moved_act, 1)
                    if ahead:
                        (sigmoids if g_ahead else softmax)(*ahead)
                    if u == MOVE_LAST_AT and later(h, 1):
                        move_o(h - 1, 1)
                    if u == MOVE_AT:
                        move_o(h, 0)
                    if u in PREP_AT and following:
                        prep(*following, PREP_AT[u])

            def start():
                for m in range(4):
                    prep(0, 0, m)
                for u in range(AHEAD):
                    softmax(0, 0, u)

            run_pairs(act, start, pair)
            move_o(NHEAD - 1, 1)

        def dve_prompt(dve):
            dve.wait_ge(qs_zero, 1)
            for g in range(2):
                dve.wait_ge(sn_ready, 2 * g + 1)
                for hh in range(2):
                    src = bank[hh * HD:hh * HD + HD, 4 + g, :].rearrange("p (j b s) -> p b j s", j=NPAIR, b=DB)
                    mv = dve.tensor_copy(qs[hh * HD:hh * HD + HD, g, :, :, hh * DS:hh * DS + DS], src)
                mv.then_inc(sn_moved, 1)
                dve.wait_ge(sn_ready, 2 * g + 2)
                dve.tensor_copy(flat(kns[:, g]), bank[:, 6 + g, :]).then_inc(sn_moved, 1)
            for c in range(4):
                dve.wait_ge(lc_ready, c + 1)
                dst = cT[:, 0:PAST].rearrange("m (p j) -> m j p", j=4 * CH)[:, 4 * c:4 * c + 4, :]
                dve.tensor_copy(dst, bank[0:DB * H, c, :].rearrange("m (j p) -> m j p", j=4)).then_inc(lc_moved, 1)

            def prep(p, hh, m):
                h, (kind, seg) = head_of(p, hh), PREP[m]
                dve.wait_ge(prep_hi, 4 * h + m + 1)
                cols = slice(512 * seg, 512 * seg + 512)
                if kind == "q":
                    dve.tensor_tensor(q_ll[:, hh, cols], bank[:, MI, :], q_hh[:, hh, cols].bitcast(F32),
                                      ALU.subtract).then_inc(prep_done, 1)
                else:
                    dve.tensor_tensor(k_hl[HD:P, hh, cols], bank[HD:P, MI, :],
                                      k_hl[HD:P, hh, cols].bitcast(F32), ALU.subtract).then_inc(prep_done, 1)

            def maxima(p, hh, u):
                k, n = unit_of(p, hh, u), (TP - u) * P
                if u == 0:
                    dve.wait_ge(cb_loaded[hh], 16 * (p + 1))
                wait_unit_free(dve, p, hh, u)
                plain_wait(dve, sc_ready, k + 1)
                dve.tensor_tensor_reduce(pr[:, u % 4, 0:n], sc_view(u, n), c_b[:, hh, 0:n],
                                         1.0, LOWEST, ALU.add, ALU.max, rowmax[:, u % 4:u % 4 + 1]).then_inc(s_moved, 1)
                dve.wait_ge(s_moved, k + 1)
                dve.tensor_scalar(negmax[:, u % 4:u % 4 + 1], rowmax[:, u % 4:u % 4 + 1], -SCALE, None, ALU.mult
                                  ).then_inc(negmax_ready, 1)

            def scans(p, hh, u):
                k, n = unit_of(p, hh, u), (TP - u) * P
                dve.wait_ge(sig_step, k - 63)
                x = om[:, u % 4, 0:n][:, ::-1]
                dve.tensor_tensor_scan(x, x, x, 1.0, ALU.mult, ALU.bypass).then_inc(scan_done, 1)

            def store_o(p, hh, half, g):
                h, base = head_of(p, hh), 4 - 4 * half
                if not g:
                    dve.wait_ge(pf_ready, NU * h + 4 * half + 4)
                    if later(h, 1):
                        dve.wait_ge(on_done, 2 * h + half)
                    dve.reciprocal(rowinv[:, base:base + 4, hh], rowsum[:, base:base + 4, hh]).then_inc(rinv_done, 1)
                    dve.wait_ge(rinv_done, 2 * h + half + 1)
                dve.wait_ge(otr_ready, 2 * h + half + 1)
                dst = o_nat[:, base:base + 4, bass.ds(p * P + hh * HD, HD)]
                src = bank[:, MI, 0:4 * HD].rearrange("p (t d) -> p t d", t=4)
                if g:
                    dve.tensor_copy(dst, src).then_inc(on_done, 1)
                else:
                    inv = rowinv[:, base:base + 4, hh].unsqueeze(2).to_broadcast([P, 4, HD])
                    dve.tensor_tensor(dst, src, inv, ALU.mult).then_inc(on_done, 1)

            def pair(p, g, g_next):
                for hh, u, ahead, g_ahead, following in steps(p, g, g_next):
                    if ahead and not g_ahead:
                        maxima(*ahead)
                    for n in range(TRB[u]):
                        if g or (TRA[u] + n) % 2 == 1:
                            dve.tensor_copy(*move_pt(dve, p, hh, u, n)).then_inc(pt_moved_dve, 1)
                    if ahead and g_ahead:
                        scans(*ahead)
                    if u == TURN_LAST_AT:
                        if hh:
                            store_o(p, 0, 1, g)
                        elif later(p, 1):
                            store_o(p - 1, 1, 1, int(g and not (isinstance(p, int) and p == NPAIR)))
                    if u == TURN_AT:
                        store_o(p, hh, 0, g)
                    if u in PREP_AT and following:
                        prep(*following, PREP_AT[u])

            def start():
                for m in range(4):
                    prep(0, 0, m)
                for u in range(AHEAD):
                    maxima(0, 0, u)
                dve.wait_ge(ln_loaded, 16 * DB)
                dve.wait_ge(lc_moved, 4)
                dve.tensor_tensor_scan(cT8, cT, cT, 0.0, ALU.add, ALU.bypass).then_inc(ct_step, 1)
                dve.wait_ge(ct_step, 1)
                dve.tensor_scalar(cT8, cT8, -1.0 / SCALE, None, ALU.mult).then_inc(ct_step, 1)

            run_pairs(dve, start, pair)
            store_o(2 * NPAIR - 1, 1, 1, 1)

        def pool_prompt(pool):
            pool.wait_ge(lc_loaded, 16)
            pool.tensor_copy(l_nat.rearrange("p j (b h) -> p j b h", b=DB),
                             l_in.rearrange("p (b j h) -> p j b h", b=DB, h=H)).then_inc(lc_sorted, 1)
            with pool.Fori(8, NHEAD) as h:
                for u in range(NU):
                    n, k = (TP - u) * P, NU * h + u
                    pool.wait_ge(scan_done, k - 63)
                    pool.wait_ge(s_moved, k + 1)
                    x = pr[:, u % 4, 0:n - 1]
                    pool.tensor_tensor(x, x, om[:, u % 4, 1:n], ALU.mult).then_inc(pb_ready, 1)


        kd_loaded = [sem(f"kd_loaded{c}") for c in range(CH)]
        vd_loaded = [sem(f"vd_loaded{c}") for c in range(CH)]
        vn_loaded = sem("vn_loaded")
        chl_ready, cur_ready = sem("chl_ready"), sem("cur_ready")
        kt_ready, kt_moved_act, kt_moved_dve = sem("kt_ready"), sem("kt_moved_act"), sem("kt_moved_dve")
        dsc_ready, dsc_moved, dmax_step, dneg_ready, dinv_done = (
            sem("dsc_ready"), sem("dsc_moved"), sem("dmax_step"), sem("dneg_ready"), sem("dinv_done"))
        dsig_step, dscan_done, dpf_ready, dps_ready, dlast_zero = (
            sem("dsig_step"), sem("dscan_done"), sem("dpf_ready"), sem("dps_ready"), sem("dlast_zero"))
        dpt_ready, dpt_moved, vd_used, dpv_done = sem("dpt_ready"), sem("dpt_moved"), sem("vd_used"), sem("dpv_done")
        od_moved, dotr_ready, dot_moved = sem("od_moved"), sem("dotr_ready"), sem("dot_moved")
        K_IN = [cache_fox_k, cache_sb_k]
        V_IN = [cache_fox_v, cache_sb_v]
        NC1 = CH + 1

        def cache_chunk(cache, b, c):
            return cache[0, bass.ds(b, 1), c * 512:c * 512 + 512].rearrange("o (t p) h d -> p (o t) (h d)", p=P)

        def load_k(sp, n, g, b, c):
            if not (isinstance(n, int) and n == 0):
                sp.wait_ge(kt_ready, 16 * (n - 1) + 4 * c + 4)
            sp.dma_start(k_ring[:, c], cache_chunk(K_IN[g], b, c)).then_inc(kd_loaded[c], 16)

        def sp_decode(sp):
            def load_v(n, g):
                b = n - 8 * g
                for c in range(CH):
                    if isinstance(n, int) and n == 0:
                        if c == 0:
                            sp.wait_ge(chl_ready, 2)
                    else:
                        sp.wait_ge(vd_used, 4 * n - 3 + c)
                    sp.dma_start(v_ring[:, c], cache_chunk(V_IN[g], b, c)).then_inc(vd_loaded[c], 16)
                if not (isinstance(n, int) and n == 0):
                    sp.wait_ge(dpv_done, n)
                sp.dma_start(v_new[:], (svs if g else fvs)[bass.ds(b * DS, DS)]).then_inc(vn_loaded, 16)

            def step(n, gk, gv):
                if gk is not None:
                    for c in range(CH):
                        load_k(sp, n + 1, gk, n + 1 - 8 * gk, c)
                load_v(n, gv)

            step(0, 0, 0)
            with sp.Fori(1, 7) as n:
                step(n, 0, 0)
            step(7, 1, 0)
            with sp.Fori(8, 15) as n:
                step(n, 1, 1)
            step(15, None, 1)

        def decode_steps(eng, logits, outputs):
            logits(0, 0)
            logits(1, 0)
            outputs(0, 0)
            with eng.Fori(2, 8) as n:
                logits(n, 0)
                outputs(n - 1, 0)
            logits(8, 1)
            outputs(7, 0)
            with eng.Fori(9, 16) as n:
                logits(n, 1)
                outputs(n - 1, 1)
            outputs(15, 1)

        def pe_decode(pe):
            def turn_keys(n, c):
                pe.wait_ge(kd_loaded[c], 16 * (n + 1))
                for j in range(NPAIR):
                    if c or not (isinstance(n, int) and n == 0):
                        pe.wait_ge(kt_moved_dve if j % 2 else kt_moved_act, 8 * n + 2 * (c - 1) + j // 2 + 1)
                    for t in range(4):
                        mm = pe.transpose(bank[:, j, t * P:t * P + P], k_ring[:, c, t, j * P:j * P + P], ident[:])
                    mm.then_inc(kt_ready, 1)

            def dot(n, c, g):
                out = bank[:, DSC + c % 2, :] if c < CH else bank[:, DNEW, 0:DS]
                cols = slice(c * 512, c * 512 + 512) if c < CH else slice(PAST, KEYS)
                if c == 0:
                    pe.wait_ge(cur_ready, 3 * n + 3 if g == 0 else 8 + 2 * n + 2)
                    if isinstance(n, int) and n == 0:
                        pe.wait_ge(chl_ready, 2)
                if c < CH:
                    if c >= 2:
                        pe.wait_ge(dsc_moved, NC1 * n + c - 1)
                    elif not (isinstance(n, int) and n == 0):
                        pe.wait_ge(dsc_moved, NC1 * n - 2 + c - 1)
                    pe.wait_ge(kt_moved_act, 8 * n + 2 * c + 2)
                    pe.wait_ge(kt_moved_dve, 8 * n + 2 * c + 2)
                else:
                    pe.matmul(out, tselb[:], mask[g][0:DS, 0:DS], start=True, stop=False, skip_group_check=True)
                if g == 0:
                    pe.matmul(out, pick_cur[:], c_hl[:, cols], start=(c < CH), stop=False, skip_group_check=True)
                for j in range(NPAIR):
                    rhs = kT[:, c % 2, j, :] if c < CH else kn_cur[:, j, :]
                    mm = pe.matmul(out[2 * DS * j:2 * DS * j + 2 * DS], q_cur[:, j, :], rhs,
                                   start=(g == 1 and c < CH), stop=True, skip_group_check=True)
                mm.then_inc(dsc_ready, 1)

            def logits(n, g):
                turn_keys(n, 0)
                turn_keys(n, 1)
                dot(n, 0, g)
                turn_keys(n, 2)
                dot(n, 1, g)
                turn_keys(n, 3)
                for c in range(2, NC1):
                    dot(n, c, g)

            def outputs(m, g):
                pe.wait_ge(dps_ready if g else dpf_ready, m + 1 - 8 * g)
                last = isinstance(m, int) and m == 15
                pe.wait_ge(kt_moved_act, 8 * m + (8 if last else 16))
                pe.wait_ge(kt_moved_dve, 8 * m + (8 if last else 16))
                for c in range(CH):
                    for t in range(4):
                        at = (4 * c + t) * P
                        mm = pe.transpose(bank[:, c, t * P:t * P + P], d_p[:, at:at + P], ident[:])
                    mm.then_inc(dpt_ready, 1)
                pe.wait_ge(dsc_moved, NC1 * (m + (1 if last else 2)))
                pe.transpose(bank[0:DS, DNEW, P:2 * P], d_p[:, PAST:KEYS], ident[:]).then_inc(dpt_ready, 1)
                if isinstance(m, int) and m == 0:
                    pe.wait_ge(on_done, 2 * NHEAD)
                else:
                    pe.wait_ge(dot_moved, m)
                for c in range(CH):
                    pe.wait_ge(dpt_moved, NC1 * m + c + 1)
                    pe.wait_ge(vd_loaded[c], 16 * (m + 1))
                    for t in range(4):
                        for j in range(NPAIR):
                            mm = pe.matmul(bank[2 * DS * j:2 * DS * j + 2 * DS, MIX, 0:P],
                                           d_pT[:, 4 * c + t, 2 * DS * j:2 * DS * j + 2 * DS], v_ring[:, c, t, j * P:j * P + P],
                                           start=(c == 0 and t == 0), stop=False, skip_group_check=True)
                    mm.then_inc(vd_used, 1)
                pe.wait_ge(vn_loaded, 16 * (m + 1))
                plain_wait(pe, dpt_moved, NC1 * m + NC1)
                for j in range(NPAIR):
                    mm = pe.matmul(bank[2 * DS * j:2 * DS * j + 2 * DS, MIX, 0:P], d_pTn[:, 2 * DS * j:2 * DS * j + 2 * DS],
                                   v_new[:, j * P:j * P + P], start=False, stop=True, skip_group_check=True)
                mm.then_inc(dpv_done, 1)
                pe.wait_ge(od_moved, m + 1)
                pe.transpose(bank[:, MIX, P:2 * P], o_d[:], ident[:]).then_inc(dotr_ready, 1)

            decode_steps(pe, logits, outputs)

        def key_move(eng, n, c, j):
            eng.wait_ge(kt_ready, 16 * n + 4 * c + j + 1)
            if c >= 2:
                eng.wait_ge(dsc_ready, NC1 * n + c - 1)
            elif not (isinstance(n, int) and n == 0):
                eng.wait_ge(dsc_ready, NC1 * n - 2 + c)
            return kT[:, c % 2, j, :], bank[:, j, :]

        def logit_bank(c):
            return bank[:, DSC + c % 2, :] if c < CH else bank[:, DNEW, 0:DS]

        def logit_cols(c):
            return slice(c * 512, c * 512 + 512) if c < CH else slice(PAST, KEYS)

        def is_first(n):
            return isinstance(n, int) and n == 0

        def act_decode(act):
            act.wait_ge(otr_ready, 2 * NHEAD)

            def keys(n, c):
                for j in (0, 2):
                    act.activation(*key_move(act, n, c, j), ACT.Copy).then_inc(kt_moved_act, 1)

            def sigmoids(n, c):
                act.wait_ge(dsc_ready, NC1 * n + c + 1)
                if c == 0:
                    if isinstance(n, int):
                        act.wait_ge(dpf_ready, 8)
                    else:
                        act.wait_ge(dps_ready, n - 8)
                act.activation(d_om[:, logit_cols(c)], logit_bank(c), ACT.Sigmoid, scale=-SCALE).then_inc(dsig_step, 1)
                act.activation(d_s[:, logit_cols(c)], logit_bank(c), ACT.Sigmoid, scale=SCALE).then_inc(dsc_moved, 1)

            def logits(n, g):
                keys(n, 0)
                keys(n, 1)
                if g:
                    sigmoids(n, 0)
                keys(n, 2)
                if g:
                    sigmoids(n, 1)
                keys(n, 3)
                if g:
                    for c in range(2, NC1):
                        sigmoids(n, c)
                else:
                    act.wait_ge(dneg_ready, n + 1)
                    if not is_first(n):
                        act.wait_ge(dinv_done, n)
                        act.wait_ge(dpt_ready, NC1 * n)
                    act.activation(d_p[:], d_s[:], ACT.Exp, bias=d_neg[:, 0:1], scale=SCALE, accum_out=d_sum[:]
                                   ).then_inc(dpf_ready, 1)

            decode_steps(act, logits, lambda m, g: None)

        def dve_decode(dve):
            dve.wait_ge(otr_ready, 2 * NHEAD)
            dve.wait_ge(ct_step, 2)
            dve.tensor_copy(c_hl[0:DB * H], cT8).then_inc(chl_ready, 1)
            dve.wait_ge(chl_ready, 1)
            dve.tensor_tensor(c_hl[DB * H:P], cT8, c_hl[0:DB * H].bitcast(F32), ALU.subtract).then_inc(chl_ready, 1)

            def keys(n, c):
                for j in (1, 3):
                    dve.tensor_copy(*key_move(dve, n, c, j)).then_inc(kt_moved_dve, 1)

            def maxima(n, c):
                if c == 0 and not is_first(n):
                    dve.wait_ge(dpf_ready, n)
                plain_wait(dve, dsc_ready, NC1 * n + c + 1)
                w = 512 if c < CH else DS
                dve.tensor_tensor_reduce(d_s[:, logit_cols(c)], logit_bank(c), zero[:, 0:1].to_broadcast([P, w]),
                                         1.0, LOWEST, ALU.add, ALU.max, d_max[:, c:c + 1]).then_inc(dsc_moved, 1)

            def logits(n, g):
                keys(n, 0)
                keys(n, 1)
                if not g:
                    maxima(n, 0)
                keys(n, 2)
                if not g:
                    maxima(n, 1)
                keys(n, 3)
                if not g:
                    for c in range(2, NC1):
                        maxima(n, c)
                    dve.wait_ge(dsc_moved, NC1 * n + NC1)
                    dve.tensor_reduce(d_max[:, NC1:NC1 + 1], d_max[:, 0:NC1], AX.X, ALU.max).then_inc(dmax_step, 1)
                    dve.wait_ge(dmax_step, n + 1)
                    dve.tensor_scalar(d_neg[:], d_max[:, NC1:NC1 + 1], -SCALE, None, ALU.mult).then_inc(dneg_ready, 1)

            def outputs(m, g):
                if g == 0:
                    dve.wait_ge(dpf_ready, m + 1)
                    if not is_first(m):
                        dve.wait_ge(od_moved, m)
                    dve.reciprocal(d_inv[:], d_sum[:]).then_inc(dinv_done, 1)
                for c in range(NC1):
                    dve.wait_ge(dpt_ready, NC1 * m + c + 1)
                    if c == 0 and not is_first(m):
                        dve.wait_ge(dpv_done, m)
                    if c < CH:
                        dve.tensor_copy(flat(d_pT[:, 4 * c:4 * c + 4, :]), bank[:, c, :]).then_inc(dpt_moved, 1)
                    else:
                        dve.tensor_copy(d_pTn[:], bank[0:DS, DNEW, P:2 * P]).then_inc(dpt_moved, 1)
                n = m + 1
                if not isinstance(n, int) or n < 16:
                    if g == 1 or (isinstance(m, int) and m == 7):
                        scan(n)
                dve.wait_ge(dpv_done, m + 1)
                if not is_first(m):
                    dve.wait_ge(dotr_ready, m)
                if g == 0:
                    dve.wait_ge(dinv_done, m + 1)
                    dve.tensor_scalar(o_d[:], bank[:, MIX, 0:P], d_inv[:, 0:1], None, ALU.mult).then_inc(od_moved, 1)
                else:
                    dve.tensor_copy(o_d[:], bank[:, MIX, 0:P]).then_inc(od_moved, 1)
                dve.wait_ge(dotr_ready, m + 1)
                for hh in range(2):
                    part = slice(hh * HD, hh * HD + HD)
                    src = bank[part, MIX, P:2 * P].rearrange("p (j h s) -> p j h s", j=NPAIR, h=2)[:, :, hh, :]
                    mv = dve.tensor_copy(oT_s[part, g, :, bass.ds((m - 8 * g) * DS, DS)], src)
                mv.then_inc(dot_moved, 1)

            def scan(n):
                dve.wait_ge(dsc_moved, NC1 * n + NC1)
                x = d_om[:, ::-1]
                dve.tensor_tensor_scan(x, x, x, 1.0, ALU.mult, ALU.bypass).then_inc(dscan_done, 1)

            decode_steps(dve, logits, outputs)

        def pool_decode(pool):
            pool.wait_ge(otr_ready, 2 * NHEAD)
            pool.wait_ge(sn_moved, 4)

            def current(n, g):
                b = n - 8 * g
                if not is_first(n):
                    pool.wait_ge(dsc_ready, NC1 * n)
                pool.tensor_copy(q_cur[:], qs[:, g, bass.ds(b, 1)].rearrange("p o j m -> p (o j) m")).then_inc(cur_ready, 1)
                pool.tensor_copy(kn_cur[:], kns[:, g, :, bass.ds(b * DS, DS)]).then_inc(cur_ready, 1)
                if g == 0:
                    pool.tensor_copy(pick_cur[:], pickf[:, bass.ds(b, 1)].rearrange("p o m -> p (o m)")).then_inc(cur_ready, 1)

            def product(n):
                pool.wait_ge(dscan_done, n - 7)
                pool.wait_ge(dpt_ready, NC1 * n)
                pool.tensor_tensor(d_p[:, 0:KEYS - 1], d_s[:, 0:KEYS - 1], d_om[:, 1:KEYS], ALU.mult).then_inc(dps_ready, 1)

            current(0, 0)
            with pool.Fori(1, 8) as n:
                current(n, 0)
            current(8, 1)
            pool.wait_ge(dpt_ready, NC1 * 8)
            pool.memset(d_p[:, KEYS - 1:KEYS], 0.0).then_inc(dlast_zero, 1)
            product(8)
            with pool.Fori(9, 16) as n:
                current(n, 1)
                product(n)

        b_loaded = sem("b_loaded")
        wr_loaded = [sem(f"wr_loaded{c}") for c in range(4)]
        wohi_done, wolo_done = sem("wohi_done"), sem("wolo_done")
        z_loaded, xm_loaded = [sem("z_loaded0"), sem("z_loaded1")], [sem("xm_loaded0"), sem("xm_loaded1")]
        so_ready, so_moved = sem("so_ready"), sem("so_moved")
        msq_done, mms_done, mroot_done = sem("msq_done"), sem("mms_done"), sem("mroot_done")
        sg_done, zg_done, zs_done = sem("sg_done"), sem("zg_done"), sem("zs_done")
        y_ready, ytp_ready, yhi_done, ylo_done = sem("y_ready"), sem("ytp_ready"), sem("yhi_done"), sem("ylo_done")
        m_ready, xo_done, xsq_done, xms_done, xroot_done = (
            sem("m_ready"), sem("xo_done"), sem("xsq_done"), sem("xms_done"), sem("xroot_done"))
        yo_done, y_stored = sem("yo_done"), sem("y_stored")
        w_in_ring = k_ring[:, :, :, :].rearrange("p a b c -> p (a b c)").rearrange("p (k e) -> p k e", k=KD)
        OB = 2

        def sp_merge(sp):
            for c in range(4):
                sp.wait_ge(kt_ready, 16 * 16)
                sp.dma_start(w_in_ring[:, 2 * c:2 * c + 2, :], wo_v[:, 2 * c:2 * c + 2, :]).then_inc(wr_loaded[c], 16)
            sp.wait_ge(dot_moved, 16)
            sp.wait_ge(so_moved, 2)
            sp.dma_start(gn_b[:, 0:W], out_norm_a.to_broadcast([P, W])).then_inc(b_loaded, 16)
            sp.dma_start(gn_b[:, W:D], out_norm_b.to_broadcast([P, W])).then_inc(b_loaded, 16)
            sp.dma_start(fg_b[:], final_norm_g.rearrange("(o d) -> o d", o=1).to_broadcast([P, D])).then_inc(b_loaded, 16)

            def load_z(t, par):
                if not isinstance(t, int) or t >= 2:
                    sp.wait_ge(y_ready, 2 * (t - 1))
                sp.dma_start(zt[:, par], z_d[bass.ds(t * P, P)]).then_inc(z_loaded[par], 16)

            def load_x(t, par):
                if not isinstance(t, int) or t >= 2:
                    sp.wait_ge(xo_done, t - 1)
                src = xs_v if isinstance(t, int) and t == TP else x_prompt[0, bass.ds(t * P, P)]
                sp.dma_start(xt[:, par], src).then_inc(xm_loaded[par], 16)

            def store(t):
                sp.wait_ge(yo_done, t + 1)
                dst = ys_v if isinstance(t, int) and t == TP else y_prompt[0, bass.ds(t * P, P)]
                sp.dma_start(dst, o_nat[:, bass.ds(t, 1)].rearrange("p o d -> p (o d)")).then_inc(y_stored, 16)

            load_z(0, 0)
            load_z(1, 1)
            load_x(0, 0)
            load_x(1, 1)
            load_z(2, 0)
            with sp.Fori(1, TP // 2) as t2:
                for par in range(2):
                    load_z(2 * t2 + par + 1, 1 - par)
                    load_x(2 * t2 + par, par)
                    store(2 * t2 + par - 2)
            load_x(TP, 0)
            for t in range(TP - 2, T):
                store(t)
            sp.wait_ge(y_stored, 16 * T)

        def act_merge(act):
            for c in range(4):
                act.wait_ge(wr_loaded[c], 16)
                if c == 0:
                    act.wait_ge(dps_ready, 8)
                act.activation(wo_hi[:, 2 * c:2 * c + 2, :], w_in_ring[:, 2 * c:2 * c + 2, :], ACT.Copy).then_inc(wohi_done, 1)
            act.wait_ge(so_moved, 2)

            def front(t, par):
                if not is_first(t):
                    act.wait_ge(msq_done, 2 * t)
                if not (isinstance(t, int) and t < 3):
                    act.wait_ge(xsq_done, t - 2)
                for g in range(2):
                    act.activation(junk[:, g * W:g * W + W], row(o_nat[:, :, g * W:g * W + W], t), ACT.Square,
                                   accum_out=row(m_stat[:, 0, :, g:g + 1], t)).then_inc(msq_done, 1)
                act.wait_ge(z_loaded[par], front_loads(t, par))
                if not is_first(t):
                    act.wait_ge(zs_done, t)
                act.activation(sg[:], zt[:, par], ACT.Sigmoid).then_inc(sg_done, 1)
                for b in range(2):
                    act.wait_ge(ytp_ready, 2 * t + b + 1)
                    if b == 0 and not (isinstance(t, int) and t < 2):
                        act.wait_ge(m_ready, 2 * (t - 1))
                    act.activation(yT_hi[:, par, 4 * b:4 * b + 4, :], bank[:, b, :].rearrange("p (k s) -> p k s", k=4),
                                   ACT.Copy).then_inc(yhi_done, 1)

            def back(t, par):
                act.wait_ge(xo_done, t + 1)
                act.wait_ge(msq_done, min(2 * (t + 3), 2 * T) if isinstance(t, int) else 2 * (t + 3))
                act.activation(junk[:], row(o_nat, t), ACT.Square, accum_out=row(m_stat[:, 0, :, 2:3], t)
                               ).then_inc(xsq_done, 1)

            merge_order(act, front, back)

        def merge_order(eng, front, back, lag=1):
            def step(t, par):
                if not isinstance(t, int) or t < T:
                    front(t, par)
                if not isinstance(t, int) or t > lag:
                    back(t - 1 - lag, (par + 1 + lag) % 2)

            for t in range(3):
                step(t, t % 2)
            with eng.Fori(1, TP // 2) as t2:
                half[0] = t2
                step(2 * t2 + 1, 1)
                step(2 * t2 + 2, 0)
            for t in range(T, T + 1 + lag):
                step(t, t % 2)

        half = [None]

        def front_loads(t, par):
            return 16 * (t // 2 + 1) if isinstance(t, int) else 16 * (half[0] + (1 if par else 2))

        def back_loads(t, par):
            return 16 * (t // 2 + 1) if isinstance(t, int) else 16 * (half[0] + (0 if par else 1))

        def row(ap, t):
            return ap[:, bass.ds(t, 1)].rearrange("p o d -> p (o d)")

        def dve_merge(dve):
            for c in range(4):
                dve.wait_ge(wohi_done, c + 1)
                dve.tensor_tensor(wo_lo[:, 2 * c:2 * c + 2, :], w_in_ring[:, 2 * c:2 * c + 2, :],
                                  wo_hi[:, 2 * c:2 * c + 2, :].bitcast(F32), ALU.subtract).then_inc(wolo_done, 1)
            for g in range(2):
                dve.wait_ge(so_ready, g + 1)
                dve.tensor_copy(o_nat[:, TP, g * W:g * W + W], bank[:, g, :]).then_inc(so_moved, 1)

            def front(t, par):
                dve.wait_ge(msq_done, 2 * t + 2)
                dve.tensor_scalar(row(m_stat[:, 1, :, 0:2], t), row(m_stat[:, 0, :, 0:2], t), 1.0 / W, EPS, ALU.mult, ALU.add
                                  ).then_inc(mms_done, 1)
                dve.wait_ge(mroot_done, t + 1)
                dve.wait_ge(zs_done, t + 1)
                if not is_first(t):
                    dve.wait_ge(ytp_ready, 2 * t)
                for g in range(2):
                    dve.scalar_tensor_tensor(out=yg[:, g * W:g * W + W], in0=row(o_nat[:, :, g * W:g * W + W], t),
                                             scalar=row(m_stat[:, 2, :, g:g + 1], t), in1=zt[:, par, g * W:g * W + W],
                                             op0=ALU.mult, op1=ALU.mult).then_inc(y_ready, 1)
                for b in range(2):
                    dve.wait_ge(yhi_done, 2 * t + b + 1)
                    dve.tensor_tensor(yT_lo[:, par, 4 * b:4 * b + 4, :], bank[:, b, :].rearrange("p (k s) -> p k s", k=4),
                                      yT_hi[:, par, 4 * b:4 * b + 4, :].bitcast(F32), ALU.subtract).then_inc(ylo_done, 1)

            def back(t, par):
                dve.wait_ge(m_ready, 2 * t + 2)
                dve.wait_ge(xm_loaded[par], back_loads(t, par))
                dve.tensor_tensor(row(o_nat, t), flat(bank[:, OB + 2 * par:OB + 2 * par + 2, :]), xt[:, par], ALU.add
                                  ).then_inc(xo_done, 1)
                dve.wait_ge(xsq_done, t + 1)
                dve.tensor_scalar(row(m_stat[:, 1, :, 2:3], t), row(m_stat[:, 0, :, 2:3], t), 1.0 / D, EPS, ALU.mult, ALU.add
                                  ).then_inc(xms_done, 1)
                dve.wait_ge(xroot_done, t + 1)
                dve.scalar_tensor_tensor(out=row(o_nat, t), in0=row(o_nat, t), scalar=row(m_stat[:, 2, :, 2:3], t),
                                         in1=fg_b[:], op0=ALU.mult, op1=ALU.mult).then_inc(yo_done, 1)

            dve.wait_ge(b_loaded, 48)
            merge_order(dve, front, back)

        def pool_merge(pool):
            pool.wait_ge(b_loaded, 48)

            def front(t, par):
                pool.wait_ge(mms_done, t + 1)
                pool.tensor_tensor(row(m_stat[:, 2, :, 0:2], t), row(m_stat[:, 1, :, 0:2], t), neghalf[:, 0:2], ALU.pow
                                   ).then_inc(mroot_done, 1)
                pool.wait_ge(sg_done, t + 1)
                pool.tensor_tensor(zt[:, par], zt[:, par], gn_b[:], ALU.mult).then_inc(zg_done, 1)
                pool.wait_ge(zg_done, t + 1)
                pool.tensor_tensor(zt[:, par], zt[:, par], sg[:], ALU.mult).then_inc(zs_done, 1)

            def back(t, par):
                pool.wait_ge(xms_done, t + 1)
                pool.tensor_tensor(row(m_stat[:, 2, :, 2:3], t), row(m_stat[:, 1, :, 2:3], t), neghalf[:, 0:1], ALU.pow
                                   ).then_inc(xroot_done, 1)

            merge_order(pool, front, back)

        def pe_merge(pe):
            pe.wait_ge(dot_moved, 16)
            for g in range(2):
                for j in range(NPAIR):
                    mm = pe.transpose(bank[:, g, j * P:j * P + P], oT_s[:, g, j, :], ident[:])
                mm.then_inc(so_ready, 1)

            def front(t, par):
                pe.wait_ge(y_ready, 2 * t + 2)
                if is_first(t):
                    pe.wait_ge(so_moved, 2)
                else:
                    pe.wait_ge(ylo_done, 2 * t)
                for b in range(2):
                    for k in range(4):
                        mm = pe.transpose(bank[:, b, k * P:k * P + P], yg[:, (4 * b + k) * P:(4 * b + k) * P + P], ident[:])
                    mm.then_inc(ytp_ready, 1)

            def back(t, par):
                pe.wait_ge(ylo_done, 2 * t + 2)
                if not (isinstance(t, int) and t < 2):
                    pe.wait_ge(xo_done, t - 1)
                if is_first(t):
                    pe.wait_ge(wolo_done, 4)
                for half_ in range(2):
                    cols = slice(half_ * W, half_ * W + W)
                    for k in range(KD):
                        for n, (a, b) in enumerate(((yT_hi, wo_hi), (yT_hi, wo_lo), (yT_lo, wo_hi))):
                            mm = pe.matmul(bank[:, OB + 2 * par + half_, :], a[:, par, k, :], b[:, k, cols],
                                           start=(k == 0 and n == 0), stop=(k == KD - 1 and n == 2))
                    mm.then_inc(m_ready, 1)

            merge_order(pe, front, back, lag=0)

        block_ = keep.enter_context(nc.Block())

        @block_.gpsimd
        def _(pool):
            pool.memset(ident[:], 0.0).then_inc(pool_step, 1)
            pool.memset(neghalf[:], -0.5).then_inc(pool_step, 1)
            pool.wait_ge(pool_step, 2)
            pool.affine_select(out=ident[:], in_=ident[:], compare_op=ALU.not_equal, fill=1.0, base=0,
                               pattern=[[-1, P]], channel_multiplier=1).then_inc(consts, 1)
            pool.memset(identb[:], 0.0).then_inc(pool_step, 1)
            pool.memset(mask[0][:], 0.0).then_inc(pool_step, 1)
            pool.memset(mask[1][:], 0.0).then_inc(pool_step, 1)
            pool.memset(tselb[:], 0.0).then_inc(pool_step, 1)
            pool.memset(zero[:], 0.0).then_inc(pool_step, 1)
            pool.memset(pickf[:], 0.0).then_inc(pool_step, 1)
            pool.wait_ge(pool_step, 8)
            pool.affine_select(out=identb[:], in_=identb[:], compare_op=ALU.not_equal, fill=1.0, base=0,
                               pattern=[[-1, P]], channel_multiplier=1).then_inc(consts, 1)
            for g in range(2):
                pool.affine_select(out=mask[g][:], in_=mask[g][:], compare_op=ALU.is_ge, fill=MASKED, base=-g,
                                   pattern=[[-1, P]], channel_multiplier=1).then_inc(consts, 1)
            pool.affine_select(out=tselb[:].rearrange("p (h t) -> p h t", h=H), in_=tselb[:].rearrange("p (h t) -> p h t", h=H),
                               compare_op=ALU.not_equal, fill=1.0, base=0, pattern=[[0, H], [-1, DS]],
                               channel_multiplier=1).then_inc(consts, 1)
            pick = pickf[:].rearrange("p b (h t) -> p b h t", h=H)
            for half in range(2):
                pool.affine_select(out=pick, in_=pick, compare_op=ALU.not_equal, fill=1.0, base=-DB * H * half,
                                   pattern=[[-H, DB], [-1, H], [0, DS]], channel_multiplier=1).then_inc(consts, 1)
                pool.wait_ge(consts, 6 + half)
            pool_project(pool)
            if stages >= 2:
                pool.memset(qs[:], 0.0).then_inc(qs_zero, 1)
                pool_prompt(pool)
            if stages >= 3:
                pool_decode(pool)
            if stages >= 4:
                pool_merge(pool)

        @block_.sync
        def _(sp):
            sp_project(sp)
            if stages >= 2:
                sp_prompt(sp)
            if stages >= 3:
                sp_decode(sp)
            if stages >= 4:
                sp_merge(sp)

        @block_.scalar
        def _(act):
            act_project(act)
            if stages >= 2:
                act_prompt(act)
            if stages >= 3:
                act_decode(act)
            if stages >= 4:
                act_merge(act)

        @block_.vector
        def _(dve):
            dve_project(dve)
            if stages >= 2:
                dve_prompt(dve)
            if stages >= 3:
                dve_decode(dve)
            if stages >= 4:
                dve_merge(dve)

        @block_.tensor
        def _(pe):
            pe_project(pe)
            if stages >= 2:
                pe.wait_ge(consts, 7)
                pe_prompt(pe)
            if stages >= 3:
                pe_decode(pe)
            if stages >= 4:
                pe_merge(pe)


_INS = ["x_prompt", "x_sample", "cache_fox_k", "cache_fox_v", "cache_fox_logf", "cache_sb_k", "cache_sb_v",
        "norm_g", "w_in", "b_f", "out_norm_a", "out_norm_b", "w_out", "final_norm_g"]


def kernel(**inputs):
    import numpy as np
    import concourse.bacc as bacc
    from concourse.bass_utils import run_bass_kernel_spmd

    nc = bacc.Bacc("TRN2", target_bir_lowering=False, num_devices=1)
    arrays, args = {}, []
    for name in _INS:
        a = np.ascontiguousarray(inputs[name])
        arrays[f"in_{name}"] = a
        args.append(nc.dram_tensor(f"in_{name}", a.shape, mybir.dt.from_np(a.dtype), kind="ExternalInput").ap())
    xp, xs, kc = (inputs[n].shape for n in ("x_prompt", "x_sample", "cache_fox_k"))
    heads, hd = kc[3], kc[4]
    prompt, sample = (1, xp[0], xp[1], heads), (1, xs[0], xs[1], heads)
    shapes = [xp, xs] + [s for lead in (prompt, sample) for s in (lead + (hd,), lead + (hd,), lead, lead + (hd,), lead + (hd,))]
    for i, shape in enumerate(shapes):
        args.append(nc.dram_tensor(f"out_{i}", shape, F32, kind="ExternalOutput").ap())
    build(nc, *args)
    r = run_bass_kernel_spmd(nc, [arrays], core_ids=[0])
    return tuple(r.results[0][f"out_{i}"] for i in range(len(shapes)))
```

```python
from contextlib import ExitStack

import concourse.bass as bass
from concourse import mybir

F32 = mybir.dt.float32
F32R = mybir.dt.float32r
BF16 = mybir.dt.bfloat16
ALU = mybir.AluOpType
ACT = mybir.ActivationFunctionType
AX = mybir.AxisListType

P = 128
EPS = 1e-6
MASKED = -(2.0 ** 100)
LOWEST = -3.0e38


def build(nc, x_prompt, x_sample, cache_fox_k, cache_fox_v, cache_fox_logf, cache_sb_k, cache_sb_v,
          norm_g, w_in, b_f, out_norm_a, out_norm_b, w_out, final_norm_g,
          y_prompt, y_sample, fk_p, fv_p, ff_p, sk_p, sv_p, fk_s, fv_s, ff_s, sk_s, sv_s):
    _, SEQ, D = x_prompt.shape
    _, DB, PAST, H, HD = cache_fox_k.shape
    DS = x_sample.shape[1]
    KD = D // P
    TP = SEQ // P
    T = TP + 1
    TOK = T * P
    W = H * HD
    NPAIR = H // 2
    SCALE = HD ** -0.5
    KEYS = PAST + DS
    CH = PAST // 512
    assert (DB * DS, W, KD, TP, CH, H) == (P, 512, 8, 8, 4, 8)
    BLOCK_AT = [0, W, 2 * W, 3 * W + H, 4 * W + H, 5 * W + H, 6 * W + H, 7 * W + H]
    F_AT = 3 * W
    NB = len(BLOCK_AT)

    q_d = nc.dram_tensor("q_scratch", (TOK, 2 * W), F32).ap()
    z_d = nc.dram_tensor("z_scratch", (TOK, 2 * W), F32).ap()
    c_d = nc.dram_tensor("c_scratch", (H, SEQ), F32).ap()

    xp_v = x_prompt[0].rearrange("(t p) d -> t p d", p=P)
    xs_v = x_sample.rearrange("b s d -> (b s) d")
    w_v = w_in[0].rearrange("(k p) e -> p k e", p=P)
    wo_v = w_out[0].rearrange("(k p) e -> p k e", p=P)
    ys_v = y_sample.rearrange("b s d -> (b s) d")

    def rows(ap):
        return ap[0].rearrange("b s h d -> (b s) (h d)")

    fkp, fvp, skp, svp = rows(fk_p), rows(fv_p), rows(sk_p), rows(sv_p)
    fks, fvs, sks, svs = rows(fk_s), rows(fv_s), rows(sk_s), rows(sv_s)
    def block_rows(c, rows, sample):
        kind, g = c % 4, c // 4
        if kind in (0, 3):
            return (z_d if kind else q_d)[rows, g * W:g * W + W]
        at = [[[fkp, fks], [skp, sks]], [[fvp, fvs], [svp, svs]]][kind - 1][g][sample]
        return at if sample else at[rows]

    sems = ExitStack()

    def sem(name):
        return sems.enter_context(nc.semaphore(name))

    def allocator(stack, kind):
        make = nc.sbuf_tensor if kind == "sbuf" else nc.psum_tensor
        return lambda name, shape, dt: stack.enter_context(make(name, shape, dt))

    with sems, ExitStack() as keep:
        sb = allocator(keep, "sbuf")
        ident = sb("ident", [P, P], F32)
        identb = sb("identb", [P, P], BF16)
        mask = [sb("mask_fox", [P, P], BF16), sb("mask_sb", [P, P], BF16)]
        tselb = sb("tselb", [DS, P], BF16)
        pickf = sb("pickf", [P, DB, P], BF16)
        neghalf = sb("neghalf", [P, 2], F32)
        zero = sb("zero", [P, 1], F32)
        qs = sb("qs", [P, 2, DB, NPAIR, 2 * DS], F32)
        kns = sb("kns", [P, 2, NPAIR, P], F32)
        stat = sb("stat", [P, 64], F32)
        rowmax = sb("rowmax", [P, 4], F32)
        negmax = sb("negmax", [P, 4], F32)
        rowsum = sb("rowsum", [P, TP, 2], F32)
        rowinv = sb("rowinv", [P, TP, 2], F32)
        d_max = sb("d_max", [P, CH + 2], F32)
        d_neg = sb("d_neg", [P, 1], F32)
        d_sum = sb("d_sum", [P, 1], F32)
        d_inv = sb("d_inv", [P, 1], F32)
        m_stat = sb("m_stat", [P, 3, T, 4], F32)

        one = ExitStack()
        sb1 = allocator(one, "sbuf")
        hT_hi = sb1("hT_hi", [P, KD, TOK], F32R)
        hT_lo = sb1("hT_lo", [P, KD, TOK], F32R)
        w_hi = [sb1("w_hi0", [P, KD, W], F32R), None]
        w_lo = [sb1("w_lo0", [P, KD, W], F32R), None]
        x_in = sb1("x_in", [P, 2, D], F32)
        h_nat = sb1("h_nat", [P, D], F32)
        ng_b = sb1("ng_b", [P, D], F32)
        fx = sb1("fx", [H, TOK], F32)
        fe = sb1("fe", [H, TOK], F32)
        w_raw = sb1("w_raw", [P, 2, KD // 2, W], F32)
        w_hi[1] = sb1("w_hi1", [P, KD, W], F32R)
        w_lo[1] = sb1("w_lo1", [P, KD, W], F32R)
        u_out = sb1("u_out", [P, 3, W], F32)
        wf_raw = sb1("wf_raw", [P, KD, H], F32)
        wf_hi = sb1("wf_hi", [P, KD, H], F32R)
        wf_lo = sb1("wf_lo", [P, KD, H], F32R)
        bf_col = sb1("bf_col", [H, 1], F32)
        lfT = fe
        c8 = fx[:, 0:SEQ]
        lf_nat = sb1("lf_nat", [P, T, H], F32)
        one.close()

        sb_o = allocator(keep, "sbuf")
        o_nat = sb_o("o_nat", [P, T, D], F32)
        over = ExitStack()
        wo_hi = allocator(over, "sbuf")("wo_hi", [P, KD, D], F32R)
        over.close()
        k_ring = sb_o("k_ring", [P, CH, 4, W], F32)
        v_ring = sb_o("v_ring", [P, CH, 4, W], F32)
        c_b = k_ring[:, 0, :, :].rearrange("p a c -> p (a c)").rearrange("p (h s) -> p h s", h=2)
        scratch = v_ring[:, :, :, :].rearrange("p a b c -> p (a b c)")
        q_sn = scratch[:, 2 * W:4 * W]
        k_sn = scratch[:, 4 * W:6 * W]
        cT = scratch[0:DB * H, 6 * W:6 * W + KEYS]
        l_in = scratch[:, 6 * W + KEYS:8 * W + KEYS]
        cT8 = scratch[0:DB * H, 4 * CH * W - KEYS:4 * CH * W]

        two = ExitStack()
        sb2 = allocator(two, "sbuf")
        q_nat = sb2("q_nat", [P, TP, 2, P], F32)
        k_nat = sb2("k_nat", [P, TP, 2, P], F32)
        v_nat = sb2("v_nat", [P, TP, P], F32)
        over = ExitStack()
        l_nat = allocator(over, "sbuf")("l_nat", [P, 4 * CH, DB * H], F32)
        over.close()
        q_hh = sb2("q_hh", [P, 2, SEQ], F32R)
        q_ll = sb2("q_ll", [P, 2, SEQ], F32R)
        k_hl = sb2("k_hl", [P, 2, SEQ], F32R)
        pr = sb2("pr", [P, 4, SEQ], F32)
        om = sb2("om", [P, 4, SEQ], F32)
        pT = sb2("pT", [P, 4, 512], F32)
        oT = sb2("oT", [P, 512], F32)
        two.close()

        over = ExitStack()
        wo_raw = allocator(over, "sbuf")("wo_raw", [P, KD, D], F32)
        over.close()
        wo_lo = sb_o("wo_lo", [P, KD, D], F32R)
        three = ExitStack()
        sb3 = allocator(three, "sbuf")
        kT = sb3("kT", [P, 2, NPAIR, 512], F32)
        d_s = sb3("d_s", [P, KEYS], F32)
        over = ExitStack()
        c_hl = allocator(over, "sbuf")("c_hl", [P, KEYS], F32R)
        over.close()
        d_om = sb3("d_om", [P, KEYS], F32)
        d_p = sb3("d_p", [P, KEYS], F32)
        d_pT = sb3("d_pT", [P, 4 * CH, P], F32)
        d_pTn = sb3("d_pTn", [DS, P], F32)
        v_new = sb3("v_new", [DS, W], F32)
        q_cur = sb3("q_cur", [P, NPAIR, 2 * DS], F32)
        kn_cur = sb3("kn_cur", [P, NPAIR, DS], F32)
        pick_cur = sb3("pick_cur", [P, P], F32R)
        o_d = sb3("o_d", [P, P], F32)
        oT_s = sb3("oT_s", [P, 2, NPAIR, P], F32)
        three.close()

        four = ExitStack()
        sb4 = allocator(four, "sbuf")
        zt = sb4("zt", [P, 2, D], F32)
        xt = sb4("xt", [P, 2, D], F32)
        gn_b = sb4("gn_b", [P, D], F32)
        fg_b = sb4("fg_b", [P, D], F32)
        sb4("between1", [P, KEYS - 2 * D], F32)
        junk = sb4("junk", [P, D], F32)
        sg = sb4("sg", [P, D], F32)
        sb4("between2", [P, KEYS - 2 * D], F32)
        yg = sb4("yg", [P, D], F32)
        yT_hi = sb4("yT_hi", [P, 2, KD, P], F32R)
        yT_lo = sb4("yT_lo", [P, 2, KD, P], F32R)
        four.close()

        bank = allocator(keep, "psum")("bank", [P, 8, 512], F32)
        U, TR = 0, 4
        SC, PTB, PV, MI = 0, 4, 6, 7
        DSC, DNEW, MIX = 4, 6, 7

        def flat(ap):
            return ap.rearrange("p a b -> p (a b)")

        consts = sem("consts")
        pool_step = sem("pool_step")
        x_loaded = [sem("x_loaded0"), sem("x_loaded1")]
        g_loaded = sem("g_loaded")
        bf_loaded = sem("bf_loaded")
        wf_loaded = sem("wf_loaded")
        w_loaded = [sem("w_loaded0"), sem("w_loaded1")]
        sq_done, ms_done, rstd_done = sem("sq_done"), sem("ms_done"), sem("rstd_done")
        h_ready, htp_ready, hhi_done, hlo_done = sem("h_ready"), sem("htp_ready"), sem("hhi_done"), sem("hlo_done")
        whi_done, wlo_done = sem("whi_done"), sem("wlo_done")
        wfhi_done, wflo_done = sem("wfhi_done"), sem("wflo_done")
        u_ready, u_moved = sem("u_ready"), sem("u_moved")
        u_stored = [sem("u_stored0"), sem("u_stored1"), sem("u_stored2")]
        f_ready, f_moved, f_act, lf_done, lft_ready, lfn_done = (
            sem("f_ready"), sem("f_moved"), sem("f_act"), sem("lf_done"), sem("lft_ready"), sem("lfn_done"))
        c8_step = sem("c8_step")
        lf_stored, c8_stored = sem("lf_stored"), sem("c8_stored")

        def plain_wait(eng, semaphore, value):
            eng.wait_ge(semaphore, value)
            eng.nop(nofuse=True)

        def x_rows(t):
            return xp_v[t] if t < TP else xs_v

        def sp_project(sp):
            def load_x(t):
                if t >= 2:
                    sp.wait_ge(h_ready, t - 1)
                sp.dma_start(x_in[:, t % 2, :], x_rows(t)).then_inc(x_loaded[t % 2], 16)

            def load_w(c, half):
                if c >= 1:
                    sp.wait_ge(wlo_done, 2 * (c - 1) + half + 1)
                sp.dma_start(w_raw[:, half], w_v[:, half * 4:half * 4 + 4, BLOCK_AT[c]:BLOCK_AT[c] + W]
                             ).then_inc(w_loaded[half], 16)

            def store(c, r, s):
                sp.wait_ge(u_moved, 9 * c + 3 * r + s + 1)
                sample = isinstance(r, int) and 3 * r + s == TP
                sp.dma_start(block_rows(c, bass.ds((3 * r + s) * P, P), sample), u_out[:, s, :]).then_inc(u_stored[s], 16)

            load_x(0)
            sp.dma_start(ng_b[:], norm_g.to_broadcast([P, D])
                         ).then_inc(g_loaded, 16)
            load_w(0, 0)
            load_x(1)
            load_w(0, 1)
            sp.dma_start(wf_raw[:], w_v[:, :, F_AT:F_AT + H]).then_inc(wf_loaded, 16)
            sp.dma_start(bf_col[:], b_f.rearrange("a h -> h a")).then_inc(bf_loaded, 16)
            for t in range(2, T):
                load_x(t)
                if t == 3:
                    load_w(1, 0)
                if t == 5:
                    load_w(1, 1)
                if t >= 4:
                    store(0, (t - 4) // 3, (t - 4) % 3)
            for t in range(T - 4, T):
                store(0, t // 3, t % 3)
            load_w(2, 0)
            load_w(2, 1)
            for c in range(1, NB):
                if c == NB - 1:
                    for s in range(3):
                        sp.wait_ge(u_stored[s], 16 * 3 * c)
                    first_loads(sp)
                with sp.Fori(0, 2) as r:
                    for s in range(3):
                        store(c, r, s)
                if c < NB - 2:
                    load_w(c + 2, 0)
                for s in range(3):
                    store(c, 2, s)
                if c < NB - 2:
                    load_w(c + 2, 1)
                if c == 2:
                    sp.wait_ge(lfn_done, 1)
                    sp.dma_start(ff_p[0, 0].rearrange("(t p) h -> p t h", p=P), lf_nat[:, 0:TP, :]
                                 ).then_inc(lf_stored, 16)
                    sp.dma_start(ff_s[0].rearrange("b s h -> (b s) h"), lf_nat[:, TP, :]).then_inc(lf_stored, 16)
                    sp.wait_ge(c8_step, 2)
                    sp.dma_start(c_d, c8).then_inc(c8_stored, 16)
        def act_project(act):
            def w_split(c, half, par):
                act.wait_ge(w_loaded[half], 16 * (c + 1))
                if not isinstance(c, int) or c >= 2:
                    act.wait_ge(u_ready, 9 * (c - 1))
                act.activation(w_hi[par][:, half * 4:half * 4 + 4, :], w_raw[:, half], ACT.Copy
                               ).then_inc(whi_done, 1)

            def h_square(t):
                act.wait_ge(x_loaded[t % 2], 16 * (t // 2 + 1))
                if t >= 1:
                    act.wait_ge(htp_ready, 2 * t)
                act.activation(h_nat[:], x_in[:, t % 2, :], ACT.Square, accum_out=stat[:, t:t + 1]).then_inc(sq_done, 1)

            def h_hi(t):
                for b in range(2):
                    act.wait_ge(htp_ready, 2 * t + b + 1)
                    act.activation(hT_hi[:, 4 * b:4 * b + 4, t * P:t * P + P],
                                   bank[:, TR + b, :].rearrange("p (k s) -> p k s", k=4), ACT.Copy
                                   ).then_inc(hhi_done, 1)

            def u_move(c, t):
                act.wait_ge(u_ready, 9 * c + t + 1)
                if not isinstance(c, int) or 9 * c + t >= 3:
                    act.wait_ge(u_stored[t % 3], 16 * (3 * c + t // 3))
                act.activation(u_out[:, t % 3, :], bank[:, U + t % 3, :], ACT.Copy).then_inc(u_moved, 1)

            def block(c, par, split):
                for t in range(T):
                    u_move(c, t)
                    if split and t in (1, 4):
                        w_split(c + 1, 0 if t == 1 else 1, 1 - par)

            h_square(0)
            w_split(0, 0, 0)
            h_hi(0)
            h_square(1)
            w_split(0, 1, 0)
            h_hi(1)
            for t in range(2, T):
                h_square(t)
                h_hi(t)
                if t == 2:
                    act.wait_ge(wf_loaded, 16)
                    act.activation(wf_hi[:], wf_raw[:], ACT.Copy).then_inc(wfhi_done, 1)
                u_move(0, t - 2)
            w_split(1, 0, 1)
            w_split(1, 1, 1)
            u_move(0, T - 2)
            u_move(0, T - 1)
            block(1, 1, True)
            act.wait_ge(bf_loaded, 16)
            for m in range(3):
                act.wait_ge(f_ready, m + 1)
                act.activation(fx[:, 384 * m:384 * m + 384], bank[0:H, TR + m % 2, 0:384], ACT.Identity,
                               bias=bf_col[:, 0:1]).then_inc(f_moved, 1)
            act.wait_ge(f_moved, 3)
            act.activation(fe[:], fx[:], ACT.Abs).then_inc(f_act, 1)
            act.wait_ge(f_act, 1)
            act.activation(fe[:], fe[:], ACT.Exp, scale=-1.0).then_inc(f_act, 1)
            act.wait_ge(f_act, 2)
            act.activation(fe[:], fe[:], ACT.Ln, bias=1.0).then_inc(f_act, 1)
            with act.Fori(1, NB // 2 - 1) as c2:
                block(2 * c2, 0, True)
                block(2 * c2 + 1, 1, True)
            block(NB - 2, 0, True)
            for t in range(T):
                u_move(NB - 1, t)
                if t >= 5:
                    split_qk(act, 0, 0, t - 5)

        def dve_project(dve):
            def w_lo_part(c, half, par):
                dve.wait_ge(whi_done, 2 * c + half + 1)
                dve.tensor_tensor(w_lo[par][:, half * 4:half * 4 + 4, :], w_raw[:, half],
                                  w_hi[par][:, half * 4:half * 4 + 4, :].bitcast(F32), ALU.subtract
                                  ).then_inc(wlo_done, 1)

            def h_scale(t):
                dve.wait_ge(sq_done, t + 1)
                dve.tensor_scalar(stat[:, 16 + t:17 + t], stat[:, t:t + 1], 1.0 / D, EPS, ALU.mult, ALU.add
                                  ).then_inc(ms_done, 1)
                dve.wait_ge(rstd_done, t + 1)
                dve.scalar_tensor_tensor(out=h_nat[:], in0=x_in[:, t % 2, :], scalar=stat[:, 32 + t:33 + t],
                                         in1=ng_b[:], op0=ALU.mult, op1=ALU.mult).then_inc(h_ready, 1)

            def h_lo(t):
                for b in range(2):
                    dve.wait_ge(hhi_done, 2 * t + b + 1)
                    dve.tensor_tensor(hT_lo[:, 4 * b:4 * b + 4, t * P:t * P + P],
                                      bank[:, TR + b, :].rearrange("p (k s) -> p k s", k=4),
                                      hT_hi[:, 4 * b:4 * b + 4, t * P:t * P + P].bitcast(F32), ALU.subtract
                                      ).then_inc(hlo_done, 1)

            dve.wait_ge(g_loaded, 16)
            h_scale(0)
            w_lo_part(0, 0, 0)
            h_lo(0)
            h_scale(1)
            w_lo_part(0, 1, 0)
            h_lo(1)
            for t in range(2, T):
                h_scale(t)
                h_lo(t)
                if t == 2:
                    dve.wait_ge(wfhi_done, 1)
                    dve.tensor_tensor(wf_lo[:], wf_raw[:], wf_hi[:].bitcast(F32), ALU.subtract).then_inc(wflo_done, 1)
            for c in (1, 2):
                for half in range(2):
                    w_lo_part(c, half, c % 2)
            dve.wait_ge(f_act, 3)
            dve.scalar_tensor_tensor(out=lfT[:], in0=fx[:], scalar=0.0, in1=fe[:], op0=ALU.min, op1=ALU.subtract
                                     ).then_inc(lf_done, 1)
            dve.wait_ge(lf_done, 1)
            dve.tensor_tensor_scan(c8, lfT[:, 0:SEQ], lfT[:, 0:SEQ], 0.0, ALU.add, ALU.bypass).then_inc(c8_step, 1)
            dve.wait_ge(c8_step, 1)
            dve.tensor_scalar(c8, c8, -1.0 / SCALE, None, ALU.mult).then_inc(c8_step, 1)
            for half in range(2):
                w_lo_part(3, half, 1)
            dve.wait_ge(lft_ready, 1)
            dve.tensor_copy(flat(lf_nat[:]), bank[:, TR + 1, 0:T * H]).then_inc(lfn_done, 1)
            with dve.Fori(2, NB // 2) as c2:
                for par in range(2):
                    for half in range(2):
                        w_lo_part(2 * c2 + par, half, par)

        def pool_project(pool):
            for t in range(T):
                pool.wait_ge(ms_done, t + 1)
                pool.tensor_tensor(stat[:, 32 + t:33 + t], stat[:, 16 + t:17 + t], neghalf[:, 0:1], ALU.pow
                                   ).then_inc(rstd_done, 1)

        def pe_project(pe):
            def h_transpose(t):
                pe.wait_ge(h_ready, t + 1)
                if t >= 1:
                    pe.wait_ge(hlo_done, 2 * t)
                for b in range(2):
                    for k in range(4):
                        mm = pe.transpose(bank[:, TR + b, k * P:k * P + P], h_nat[:, (4 * b + k) * P:(4 * b + k + 1) * P],
                                          ident[:])
                    mm.then_inc(htp_ready, 1)

            def multiply(c, t, par, ks=range(KD)):
                if not isinstance(c, int) or 9 * c + t >= 3:
                    pe.wait_ge(u_moved, 9 * c + t - 2)
                for k in ks:
                    for n, (a, b) in enumerate(((hT_hi, w_hi), (hT_hi, w_lo), (hT_lo, w_hi))):
                        mm = pe.matmul(bank[:, U + t % 3, :], a[:, k, t * P:t * P + P], b[par][:, k, :],
                                       start=(k == 0 and n == 0), stop=(k == KD - 1 and n == 2))
                if ks[-1] == KD - 1:
                    mm.then_inc(u_ready, 1)

            def block(c, par):
                pe.wait_ge(wlo_done, 2 * (c + 1))
                for t in range(T):
                    multiply(c, t, par)

            pe.wait_ge(consts, 1)
            h_transpose(0)
            pe.wait_ge(hlo_done, 2)
            pe.wait_ge(wlo_done, 1)
            multiply(0, 0, 0, range(KD // 2))
            h_transpose(1)
            pe.wait_ge(wlo_done, 2)
            multiply(0, 0, 0, range(KD // 2, KD))
            for t in range(1, T):
                if t < T - 1:
                    h_transpose(t + 1)
                pe.wait_ge(hlo_done, 2 * (t + 1))
                multiply(0, t, 0)
            block(1, 1)
            pe.wait_ge(wflo_done, 1)
            for m in range(3):
                if m == 2:
                    pe.wait_ge(f_moved, 1)
                for k in range(KD):
                    for n, (a, b) in enumerate(((wf_hi, hT_hi), (wf_lo, hT_hi), (wf_hi, hT_lo))):
                        mm = pe.matmul(bank[0:H, TR + m % 2, 0:384], a[:, k, :], b[:, k, 384 * m:384 * m + 384],
                                       start=(k == 0 and n == 0), stop=(k == KD - 1 and n == 2))
                mm.then_inc(f_ready, 1)
            block(2, 0)
            pe.wait_ge(lf_done, 1)
            for t in range(T):
                mm = pe.transpose(bank[:, TR + 1, t * H:t * H + H], lfT[:, t * P:t * P + P], ident[0:H, 0:H])
            mm.then_inc(lft_ready, 1)
            block(3, 1)
            with pe.Fori(2, NB // 2 - 1) as c2:
                block(2 * c2, 0)
                block(2 * c2 + 1, 1)
            block(NB - 2, 0)
            pe.wait_ge(wlo_done, 2 * NB)
            for t in range(T):
                multiply(NB - 1, t, 1)
                pe_first(pe, t)


        AHEAD = 3
        PREP = [("k", 0), ("k", 1), ("q", 1), ("q", 0)]
        PREP_AT = {0: 0, 1: 1, 2: 2, 3: 3}
        TURN_LAST_AT, MOVE_LAST_AT, TURN_AT, MOVE_AT = 4, 1, 6, 5
        NU = TP
        NHEAD = 2 * 2 * NPAIR
        TRB = [(TP - u + 3) // 4 for u in range(NU)]
        TRA = [sum(TRB[:u]) for u in range(NU + 1)]
        NTR = TRA[NU]
        sn_loaded, lc_loaded, ln_loaded = sem("sn_loaded"), sem("lc_loaded"), sem("ln_loaded")
        cb_loaded = [sem("cb_loaded0"), sem("cb_loaded1")]
        q_loaded = [sem("q_loaded0"), sem("q_loaded1")]
        k_loaded = [sem("k_loaded0"), sem("k_loaded1")]
        v_loaded = [sem("v_loaded0"), sem("v_loaded1")]
        lc_sorted = sem("lc_sorted")
        qs_zero, sn_ready, sn_moved = sem("qs_zero"), sem("sn_ready"), sem("sn_moved")
        lc_ready, lc_moved, ct_step = sem("lc_ready"), sem("lc_moved"), sem("ct_step")
        prep_tp, prep_hi, prep_done = sem("prep_tp"), sem("prep_hi"), sem("prep_done")
        sc_ready, s_moved = sem("sc_ready"), sem("s_moved")
        negmax_ready, pf_ready = sem("negmax_ready"), sem("pf_ready")
        sig_step, scan_done, pb_ready = sem("sig_step"), sem("scan_done"), sem("pb_ready")
        pt_ready, pt_moved_act, pt_moved_dve = sem("pt_ready"), sem("pt_moved_act"), sem("pt_moved_dve")
        pv_done, ot_moved, otr_ready, rinv_done, on_done = (
            sem("pv_done"), sem("ot_moved"), sem("otr_ready"), sem("rinv_done"), sem("on_done"))

        def later(n, least):
            return not isinstance(n, int) or n >= least

        def head_of(p, hh):
            return 2 * p + hh

        def unit_of(p, hh, u):
            return 16 * p + 8 * hh + u

        def ahead_of(p, hh, u, by):
            v = u + by
            if v < NU:
                return p, hh, v
            return (p, 1, v - NU) if hh == 0 else (p + 1, 0, v - NU)

        def run_pairs(eng, start, pair):
            start()
            pair(0, 0, 0)
            with eng.Fori(1, NPAIR - 1) as p:
                pair(p, 0, 0)
            pair(NPAIR - 1, 0, 1)
            pair(NPAIR, 1, 1)
            with eng.Fori(NPAIR + 1, 2 * NPAIR - 1) as p:
                pair(p, 1, 1)
            pair(2 * NPAIR - 1, 1, None)

        def steps(p, g, g_next):
            for hh in range(2):
                for u in range(NU):
                    ahead = ahead_of(p, hh, u, AHEAD)
                    g_ahead = g_next if hh == 1 and u + AHEAD >= NU else g
                    if g_ahead is None:
                        ahead = None
                    following = (p, 1) if hh == 0 else (p + 1, 0)
                    if hh == 1 and g_next is None:
                        following = None
                    yield hh, u, ahead, g_ahead, following

        def sc_view(u, n):
            return flat(bank[:, SC + 2 * (u % 2):SC + 2 * (u % 2) + 2, :])[:, 0:n]

        def load_twice(sp, dst, src, col, hh, s):
            rows_of = src[0:SEQ, bass.ds(col + hh * HD, HD)].rearrange("(t p) d -> p t d", p=P)
            for half in range(2):
                sp.dma_start(dst[:, :, hh, half * HD:half * HD + HD], rows_of).then_inc(s[hh], 16)

        def load_qk(sp, p, hh, g):
            load_twice(sp, k_nat, skp if g else fkp, (p - NPAIR * g) * P, hh, k_loaded)
            load_twice(sp, q_nat, q_d, p * P, hh, q_loaded)

        def load_pv(sp, p, hh, g):
            src = (svp if g else fvp)[:, bass.ds((p - NPAIR * g) * P + hh * HD, HD)]
            sp.dma_start(v_nat[:, :, hh * HD:hh * HD + HD], src.rearrange("(t p) e -> p t e", p=P)
                         ).then_inc(v_loaded[hh], 16)

        def load_c(sp, p, hh):
            sp.dma_start(c_b[:, hh, :], c_d[bass.ds(head_of(p, hh), 1)].to_broadcast([P, SEQ])
                         ).then_inc(cb_loaded[hh], 16)

        def first_loads(sp):
            sp.wait_ge(lf_stored, 32)
            sp.wait_ge(c8_stored, 16)
            sp.dma_start(q_sn, q_d[SEQ:TOK, :]).then_inc(sn_loaded, 16)
            sp.dma_start(k_sn[:, 0:W], fks).then_inc(sn_loaded, 16)
            sp.dma_start(k_sn[:, W:], sks).then_inc(sn_loaded, 16)
            sp.dma_start(l_in.rearrange("p (b m) -> p b m", b=DB),
                         cache_fox_logf[0].rearrange("b (p j) h -> p b (j h)", p=P)).then_inc(lc_loaded, 16)
            for hh in range(2):
                load_qk(sp, 0, hh, 0)
            for hh in range(2):
                load_pv(sp, 0, hh, 0)
            with nc.allow_non_contiguous_dma(reason="1024 values in all"):
                for b in range(DB):
                    sp.dma_start(cT[b * H:b * H + H, PAST:KEYS], ff_s[0, b].rearrange("s h -> h s")
                                 ).then_inc(ln_loaded, 16)

        def sp_prompt(sp):
            sp.wait_ge(u_ready, 9 * NB)
            for hh in range(2):
                load_c(sp, 0, hh)
            for s in range(3):
                sp.wait_ge(u_stored[s], 16 * 3 * NB)

            def next_pair(p, g):
                for hh in range(2):
                    sp.wait_ge(prep_tp, 4 * head_of(p, hh) + 4)
                    load_qk(sp, p + 1, hh, g)
                for hh in range(2):
                    if not g:
                        sp.wait_ge(s_moved, unit_of(p, hh, NU))
                        load_c(sp, p + 1, hh)
                    sp.wait_ge(pv_done, unit_of(p, hh, NU))
                    load_pv(sp, p + 1, hh, g)

            with sp.Fori(0, NPAIR - 1) as p:
                next_pair(p, 0)
            next_pair(NPAIR - 1, 1)
            sp.wait_ge(s_moved, unit_of(NPAIR, 0, 0))
            for c in (0, 1):
                load_k(sp, 0, 0, 0, c)
            next_pair(NPAIR, 1)
            for c in (2, 3):
                load_k(sp, 0, 0, 0, c)
            with sp.Fori(NPAIR + 1, 2 * NPAIR - 1) as p:
                next_pair(p, 1)
            sp.wait_ge(ct_step, 2)
            for c in range(CH // 2):
                sp.dma_start(v_ring[:, c], cache_chunk(cache_fox_v, 0, c)).then_inc(vd_loaded[c], 16)

        def turn_qk(pe, p, hh, m):
            h, (kind, seg) = head_of(p, hh), PREP[m]
            if m == 0:
                pe.wait_ge(k_loaded[hh], 32 * (p + 1))
            if m == 2:
                pe.wait_ge(q_loaded[hh], 32 * (p + 1))
            if m:
                pe.wait_ge(prep_done, 4 * h + m)
            elif later(h, 2):
                pe.wait_ge(on_done, 2 * (h - 1) - 1)
            elif h == 1:
                pe.wait_ge(prep_done, 4)
            else:
                pe.wait_ge(lc_moved, 4)
            src = k_nat if kind == "k" else q_nat
            for t in range(4):
                mm = pe.transpose(bank[:, MI, t * P:t * P + P], src[:, 4 * seg + t, hh, :], ident[:])
            mm.then_inc(prep_tp, 1)

        def pe_first(pe, t):
            if t == 3:
                pe.wait_ge(sn_loaded, 48)
                pe.wait_ge(lfn_done, 1)
                for g in range(2):
                    for src, at in ((q_sn, 4), (k_sn, 6)):
                        for j in range(NPAIR):
                            mm = pe.transpose(bank[:, at + g, j * P:j * P + P], src[:, g * W + j * P:g * W + j * P + P], ident[:])
                        mm.then_inc(sn_ready, 1)
            if t == 4:
                pe.wait_ge(lc_sorted, 1)
                pe.wait_ge(sn_moved, 4)
                for c in range(4):
                    for j in range(4):
                        mm = pe.transpose(bank[0:DB * H, 4 + c, j * P:j * P + P], l_nat[:, 4 * c + j, :], ident[:])
                    mm.then_inc(lc_ready, 1)
            if t >= 5:
                turn_qk(pe, 0, 0, t - 5)

        def pe_prompt(pe):
            def scores(p, hh, u, g):
                k, i = unit_of(p, hh, u), TP - 1 - u
                n = (i + 1) * P
                if u == 0:
                    pe.wait_ge(prep_done, 4 * head_of(p, hh) + 4)
                if later(k, 2):
                    pe.wait_ge(s_moved, k - 1)
                else:
                    pe.wait_ge(u_moved, 9 * NB - 1 + u)
                for seg in range((n + 511) // 512):
                    w = min(512, n - seg * 512)
                    out = bank[:, SC + 2 * (u % 2) + seg, 0:w]
                    diagonal = seg == i // 4
                    for a in (q_hh, q_ll):
                        mm = pe.matmul(out, a[:, hh, i * P:i * P + P], k_hl[:, hh, seg * 512:seg * 512 + w],
                                       start=(a is q_hh), stop=(a is q_ll and not diagonal), skip_group_check=True)
                    if diagonal:
                        mm = pe.matmul(out[:, w - P:w], identb[:], mask[g][:], start=False, stop=True,
                                       skip_group_check=True)
                mm.then_inc(sc_ready, 1)

            def transpose_p(p, hh, u, g):
                k, h, i = unit_of(p, hh, u), head_of(p, hh), TP - 1 - u
                pe.wait_ge(pb_ready if g else pf_ready, k + 1 - 64 * g)
                for n in range(TRB[u]):
                    lr = TRA[u] + n
                    if g:
                        if lr == 0:
                            pe.wait_ge(pt_moved_act, NTR // 2 * 8)
                        pe.wait_ge(pt_moved_dve, NTR // 2 * 8 + NTR * (h - 8) + lr - 1)
                    elif later(h, 1) or lr >= 2:
                        pe.wait_ge(pt_moved_dve if lr % 2 else pt_moved_act, NTR // 2 * h + lr // 2)
                    else:
                        pe.wait_ge(lc_moved, 4)
                    for j in range(4 * n, min(4 * n + 4, i + 1)):
                        mm = pe.transpose(bank[:, PTB + lr % 2, (j % 4) * P:(j % 4) * P + P],
                                          pr[:, u % 4, j * P:j * P + P], ident[:])
                    mm.then_inc(pt_ready, 1)

            def outputs(p, hh, u, g):
                h, i, half = head_of(p, hh), TP - 1 - u, u // 4
                if u == 0:
                    pe.wait_ge(v_loaded[hh], 16 * (p + 1))
                if u % 4 == 0:
                    if later(h, 1):
                        pe.wait_ge(ot_moved, 2 * h - 1 + half)
                    else:
                        pe.wait_ge(lc_moved, 4)
                for j in range(i + 1):
                    lr = TRA[u] + j // 4
                    if j % 4 == 0:
                        if g:
                            pe.wait_ge(pt_moved_dve, NTR // 2 * 8 + NTR * (h - 8) + lr + 1)
                        else:
                            pe.wait_ge(pt_moved_dve if lr % 2 else pt_moved_act, NTR // 2 * h + lr // 2 + 1)
                    mm = pe.matmul(bank[half * HD:half * HD + HD, PV, (i % 4) * P:(i % 4) * P + P],
                                   v_nat[:, j, hh * HD:hh * HD + HD], pT[:, lr % 4, (j % 4) * P:(j % 4) * P + P],
                                   start=(j == 0), stop=(j == i), skip_group_check=True)
                mm.then_inc(pv_done, 1)

            def turn(h, half, last=False):
                pe.wait_ge(ot_moved, 2 * h + half + 1)
                if half and not last:
                    plain_wait(pe, prep_done, 4 * (h + 3))
                elif half or later(h, 1):
                    plain_wait(pe, on_done, 2 * h + half)
                else:
                    pe.wait_ge(prep_done, 8)
                part = slice(half * HD, half * HD + HD)
                for t in range(4):
                    mm = pe.transpose(bank[:, MI, t * HD:t * HD + HD], oT[part, t * P:t * P + P], ident[part, part])
                mm.then_inc(otr_ready, 1)

            def pair(p, g, g_next):
                for hh, u, ahead, g_ahead, following in steps(p, g, g_next):
                    h = head_of(p, hh)
                    if ahead:
                        scores(*ahead, g_ahead)
                    transpose_p(p, hh, u, g)
                    if u:
                        outputs(p, hh, u - 1, g)
                    elif hh:
                        outputs(p, 0, NU - 1, g)
                    elif later(p, 1):
                        outputs(p - 1, 1, NU - 1, int(g and not (isinstance(p, int) and p == NPAIR)))
                    if u == TURN_LAST_AT and later(h, 1):
                        turn(h - 1, 1, last=following is None)
                    if u == TURN_AT:
                        turn(h, 0, last=following is None)
                    if u in PREP_AT and following:
                        turn_qk(pe, *following, PREP_AT[u])

            def start():
                pe.wait_ge(consts, 7)
                for u in range(AHEAD):
                    scores(0, 0, u, 0)

            run_pairs(pe, start, pair)
            outputs(2 * NPAIR - 1, 1, NU - 1, 1)
            turn(NHEAD - 1, 1, last=True)

        def wait_unit_free(eng, p, hh, u):
            h = head_of(p, hh)
            if u >= 4:
                eng.wait_ge(pt_ready, NTR * h + TRA[u - 3])
            elif later(h, 1):
                eng.wait_ge(pt_ready, NTR * (h - 1) + TRA[u + 5])

        def move_pt(eng, p, hh, u, n):
            k, i = unit_of(p, hh, u), TP - 1 - u
            lr = TRA[u] + n
            w = min(4, i + 1 - 4 * n) * P
            eng.wait_ge(pt_ready, NTR * head_of(p, hh) + lr + 1)
            if later(k, 2):
                eng.wait_ge(pv_done, k - 1)
            return pT[:, lr % 4, 0:w], bank[:, PTB + lr % 2, 0:w]

        def split_qk(act, p, hh, m):
            h, (kind, seg) = head_of(p, hh), PREP[m]
            act.wait_ge(prep_tp, 4 * h + m + 1)
            if m == 0 and later(h, 2):
                act.wait_ge(sc_ready, NU * (h - 1))
            elif m == 0:
                act.wait_ge(wlo_done, 2 * NB)
            dst = k_hl if kind == "k" else q_hh
            act.activation(dst[:, hh, 512 * seg:512 * seg + 512], bank[:, MI, :], ACT.Copy).then_inc(prep_hi, 1)

        def act_prompt(act):
            def softmax(p, hh, u):
                k, h, n = unit_of(p, hh, u), head_of(p, hh), (TP - u) * P
                if u % 4 == 0 and later(h, 2):
                    act.wait_ge(rinv_done, 2 * (h - 2) + u // 4 + 1)
                act.wait_ge(negmax_ready, k + 1)
                x = pr[:, u % 4, 0:n]
                act.activation(x, x, ACT.Exp, bias=negmax[:, u % 4:u % 4 + 1], scale=SCALE,
                               accum_out=rowsum[:, TP - 1 - u, hh:hh + 1]).then_inc(pf_ready, 1)

            def sigmoids(p, hh, u):
                k, n = unit_of(p, hh, u), (TP - u) * P
                wait_unit_free(act, p, hh, u)
                act.wait_ge(sc_ready, k + 1)
                act.activation(om[:, u % 4, 0:n], sc_view(u, n), ACT.Sigmoid, scale=-SCALE).then_inc(sig_step, 1)
                act.activation(pr[:, u % 4, 0:n], sc_view(u, n), ACT.Sigmoid, scale=SCALE).then_inc(s_moved, 1)

            def move_o(h, half):
                act.wait_ge(pv_done, NU * h + 4 * half + 4)
                if later(h, 1):
                    act.wait_ge(otr_ready, 2 * h - 1 + half)
                part = slice(half * HD, half * HD + HD)
                act.activation(oT[part], bank[part, PV, :], ACT.Copy).then_inc(ot_moved, 1)

            def pair(p, g, g_next):
                for hh, u, ahead, g_ahead, following in steps(p, g, g_next):
                    h = head_of(p, hh)
                    if u - 1 in PREP_AT and following:
                        split_qk(act, *following, PREP_AT[u - 1])
                    if not g:
                        for n in range(TRB[u]):
                            if (TRA[u] + n) % 2 == 0:
                                act.activation(*move_pt(act, p, hh, u, n), ACT.Copy).then_inc(pt_moved_act, 1)
                    if u == MOVE_LAST_AT and later(h, 1):
                        move_o(h - 1, 1)
                    if u == MOVE_AT:
                        move_o(h, 0)
                    if (g_next if hh == 1 and u + AHEAD - 1 >= NU else g) == 0:
                        softmax(*ahead_of(p, hh, u, AHEAD - 1))
                    if ahead and g_ahead:
                        sigmoids(*ahead)

            def start():
                for u in range(AHEAD - 1):
                    softmax(0, 0, u)

            run_pairs(act, start, pair)
            move_o(NHEAD - 1, 1)

        def dve_prompt(dve):
            dve.wait_ge(qs_zero, 1)
            for g in range(2):
                dve.wait_ge(sn_ready, 2 * g + 1)
                for hh in range(2):
                    src = bank[hh * HD:hh * HD + HD, 4 + g, :].rearrange("p (j b s) -> p b j s", j=NPAIR, b=DB)
                    mv = dve.tensor_copy(qs[hh * HD:hh * HD + HD, g, :, :, hh * DS:hh * DS + DS], src)
                mv.then_inc(sn_moved, 1)
                dve.wait_ge(sn_ready, 2 * g + 2)
                dve.tensor_copy(flat(kns[:, g]), bank[:, 6 + g, :]).then_inc(sn_moved, 1)
            for c in range(4):
                dve.wait_ge(lc_ready, c + 1)
                dst = cT[:, 0:PAST].rearrange("m (p j) -> m j p", j=4 * CH)[:, 4 * c:4 * c + 4, :]
                dve.tensor_copy(dst, bank[0:DB * H, 4 + c, :].rearrange("m (j p) -> m j p", j=4)).then_inc(lc_moved, 1)

            def prep(p, hh, m):
                h, (kind, seg) = head_of(p, hh), PREP[m]
                dve.wait_ge(prep_hi, 4 * h + m + 1)
                cols = slice(512 * seg, 512 * seg + 512)
                if kind == "q":
                    dve.tensor_tensor(q_ll[:, hh, cols], bank[:, MI, :], q_hh[:, hh, cols].bitcast(F32),
                                      ALU.subtract).then_inc(prep_done, 1)
                else:
                    dve.tensor_tensor(k_hl[HD:P, hh, cols], bank[HD:P, MI, :],
                                      k_hl[HD:P, hh, cols].bitcast(F32), ALU.subtract).then_inc(prep_done, 1)

            def maxima(p, hh, u):
                k, n = unit_of(p, hh, u), (TP - u) * P
                if u == 0:
                    dve.wait_ge(cb_loaded[hh], 16 * (p + 1))
                wait_unit_free(dve, p, hh, u)
                plain_wait(dve, sc_ready, k + 1)
                dve.tensor_tensor_reduce(pr[:, u % 4, 0:n], sc_view(u, n), c_b[:, hh, 0:n],
                                         1.0, LOWEST, ALU.add, ALU.max, rowmax[:, u % 4:u % 4 + 1]).then_inc(s_moved, 1)
                dve.wait_ge(s_moved, k + 1)
                dve.tensor_scalar(negmax[:, u % 4:u % 4 + 1], rowmax[:, u % 4:u % 4 + 1], -SCALE, None, ALU.mult
                                  ).then_inc(negmax_ready, 1)

            def scans(p, hh, u):
                k, n = unit_of(p, hh, u), (TP - u) * P
                dve.wait_ge(sig_step, k - 63)
                x = om[:, u % 4, 0:n][:, ::-1]
                dve.tensor_tensor_scan(x, x, x, 1.0, ALU.mult, ALU.bypass).then_inc(scan_done, 1)

            def store_o(p, hh, half, g):
                h, base = head_of(p, hh), 4 - 4 * half
                if not g:
                    dve.wait_ge(pf_ready, NU * h + 4 * half + 4)
                    if later(h, 1):
                        dve.wait_ge(on_done, 2 * h + half)
                    dve.reciprocal(rowinv[:, base:base + 4, hh], rowsum[:, base:base + 4, hh]).then_inc(rinv_done, 1)
                    dve.wait_ge(rinv_done, 2 * h + half + 1)
                dve.wait_ge(otr_ready, 2 * h + half + 1)
                dst = o_nat[:, base:base + 4, bass.ds(p * P + hh * HD, HD)]
                src = bank[:, MI, 0:4 * HD].rearrange("p (t d) -> p t d", t=4)
                if g:
                    dve.tensor_copy(dst, src).then_inc(on_done, 1)
                else:
                    inv = rowinv[:, base:base + 4, hh].unsqueeze(2).to_broadcast([P, 4, HD])
                    dve.tensor_tensor(dst, src, inv, ALU.mult).then_inc(on_done, 1)

            def pair(p, g, g_next):
                for hh, u, ahead, g_ahead, following in steps(p, g, g_next):
                    for n in range(TRB[u]):
                        if g or (TRA[u] + n) % 2 == 1:
                            dve.tensor_copy(*move_pt(dve, p, hh, u, n)).then_inc(pt_moved_dve, 1)
                    if ahead:
                        (scans if g_ahead else maxima)(*ahead)
                    if u == TURN_LAST_AT:
                        if hh:
                            store_o(p, 0, 1, g)
                        elif later(p, 1):
                            store_o(p - 1, 1, 1, int(g and not (isinstance(p, int) and p == NPAIR)))
                    if u == TURN_AT:
                        store_o(p, hh, 0, g)
                    if u in PREP_AT and following:
                        prep(*following, PREP_AT[u])

            def start():
                for m in range(4):
                    prep(0, 0, m)
                for u in range(AHEAD):
                    maxima(0, 0, u)
                dve.wait_ge(ln_loaded, 16 * DB)
                dve.wait_ge(lc_moved, 4)
                dve.tensor_tensor_scan(cT8, cT, cT, 0.0, ALU.add, ALU.bypass).then_inc(ct_step, 1)
                dve.wait_ge(ct_step, 1)
                dve.tensor_scalar(cT8, cT8, -1.0 / SCALE, None, ALU.mult).then_inc(ct_step, 1)

            run_pairs(dve, start, pair)
            store_o(2 * NPAIR - 1, 1, 1, 1)

        def pool_prompt(pool):
            pool.wait_ge(lc_loaded, 16)
            pool.wait_ge(c8_stored, 16)
            pool.tensor_copy(l_nat.rearrange("p j (b h) -> p j b h", b=DB),
                             l_in.rearrange("p (b j h) -> p j b h", b=DB, h=H)).then_inc(lc_sorted, 1)
            with pool.Fori(8, NHEAD) as h:
                for u in range(NU):
                    n, k = (TP - u) * P, NU * h + u
                    pool.wait_ge(scan_done, k - 63)
                    pool.wait_ge(s_moved, k + 1)
                    x = pr[:, u % 4, 0:n - 1]
                    pool.tensor_tensor(x, x, om[:, u % 4, 1:n], ALU.mult).then_inc(pb_ready, 1)


        kd_loaded = [sem(f"kd_loaded{c}") for c in range(CH)]
        vd_loaded = [sem(f"vd_loaded{c}") for c in range(CH)]
        vn_loaded = sem("vn_loaded")
        chl_ready, cur_ready = sem("chl_ready"), sem("cur_ready")
        kt_ready, kt_moved_act, kt_moved_dve = sem("kt_ready"), sem("kt_moved_act"), sem("kt_moved_dve")
        dsc_ready, dsc_moved, dmax_step, dneg_ready, dinv_done = (
            sem("dsc_ready"), sem("dsc_moved"), sem("dmax_step"), sem("dneg_ready"), sem("dinv_done"))
        dsig_step, dscan_done, dpf_ready, dps_ready, dlast_zero = (
            sem("dsig_step"), sem("dscan_done"), sem("dpf_ready"), sem("dps_ready"), sem("dlast_zero"))
        dpt_ready, dpt_moved, vd_used, dpv_done = sem("dpt_ready"), sem("dpt_moved"), sem("vd_used"), sem("dpv_done")
        od_moved, dotr_ready, dot_moved = sem("od_moved"), sem("dotr_ready"), sem("dot_moved")
        K_IN = [cache_fox_k, cache_sb_k]
        V_IN = [cache_fox_v, cache_sb_v]
        NC1 = CH + 1

        def cache_chunk(cache, b, c):
            return cache[0, bass.ds(b, 1), c * 512:c * 512 + 512].rearrange("o (p t) h d -> p (o t) (h d)", p=P)

        def load_k(sp, n, g, b, c):
            if not (isinstance(n, int) and n == 0):
                sp.wait_ge(kt_ready, 16 * (n - 1) + 4 * c + 4)
            sp.dma_start(k_ring[:, c], cache_chunk(K_IN[g], b, c)).then_inc(kd_loaded[c], 16)

        def sp_decode(sp):
            def load_v(n, g):
                b = n - 8 * g
                for c in range(CH // 2 if is_first(n) else 0, CH):
                    if is_first(n):
                        if c == CH // 2:
                            sp.wait_ge(chl_ready, 2)
                    else:
                        sp.wait_ge(vd_used, 4 * n - 3 + c)
                    sp.dma_start(v_ring[:, c], cache_chunk(V_IN[g], b, c)).then_inc(vd_loaded[c], 16)
                if not (isinstance(n, int) and n == 0):
                    sp.wait_ge(dpv_done, n)
                sp.dma_start(v_new[:], (svs if g else fvs)[bass.ds(b * DS, DS)]).then_inc(vn_loaded, 16)

            def step(n, gk, gv):
                if gk is not None:
                    for c in range(CH):
                        load_k(sp, n + 1, gk, n + 1 - 8 * gk, c)
                load_v(n, gv)

            step(0, 0, 0)
            with sp.Fori(1, 7) as n:
                step(n, 0, 0)
            step(7, 1, 0)
            with sp.Fori(8, 15) as n:
                step(n, 1, 1)
            step(15, None, 1)

        def decode_steps(eng, logits, outputs):
            logits(0, 0)
            logits(1, 0)
            outputs(0, 0)
            with eng.Fori(2, 8) as n:
                logits(n, 0)
                outputs(n - 1, 0)
            logits(8, 1)
            outputs(7, 0)
            with eng.Fori(9, 16) as n:
                logits(n, 1)
                outputs(n - 1, 1)
            outputs(15, 1)

        def pe_decode(pe):
            def turn_keys(n, c):
                pe.wait_ge(kd_loaded[c], 16 * (n + 1))
                for j in range(NPAIR):
                    if c or not (isinstance(n, int) and n == 0):
                        pe.wait_ge(kt_moved_dve if j % 2 else kt_moved_act, 8 * n + 2 * (c - 1) + j // 2 + 1)
                    for t in range(4):
                        mm = pe.transpose(bank[:, j, t:512:4], k_ring[:, c, t, j * P:j * P + P], ident[:])
                    mm.then_inc(kt_ready, 1)

            def dot(n, c, g):
                out = bank[:, DSC + c % 2, :] if c < CH else bank[:, DNEW, 0:DS]
                cols = slice(c * 512, c * 512 + 512) if c < CH else slice(PAST, KEYS)
                if c == 0:
                    pe.wait_ge(cur_ready, 3 * n + 3 if g == 0 else 8 + 2 * n + 2)
                    if isinstance(n, int) and n == 0:
                        pe.wait_ge(chl_ready, 2)
                if c < CH:
                    if c >= 2:
                        pe.wait_ge(dsc_moved, NC1 * n + c - 1)
                    elif not (isinstance(n, int) and n == 0):
                        pe.wait_ge(dsc_moved, NC1 * n - 2 + c - 1)
                    pe.wait_ge(kt_moved_act, 8 * n + 2 * c + 2)
                    pe.wait_ge(kt_moved_dve, 8 * n + 2 * c + 2)
                else:
                    pe.matmul(out, tselb[:], mask[g][0:DS, 0:DS], start=True, stop=False, skip_group_check=True)
                if g == 0:
                    pe.matmul(out, pick_cur[:], c_hl[:, cols], start=(c < CH), stop=False, skip_group_check=True)
                for j in range(NPAIR):
                    rhs = kT[:, c % 2, j, :] if c < CH else kn_cur[:, j, :]
                    mm = pe.matmul(out[2 * DS * j:2 * DS * j + 2 * DS], q_cur[:, j, :], rhs,
                                   start=(g == 1 and c < CH), stop=True, skip_group_check=True)
                mm.then_inc(dsc_ready, 1)

            def logits(n, g):
                turn_keys(n, 0)
                turn_keys(n, 1)
                dot(n, 0, g)
                turn_keys(n, 2)
                dot(n, 1, g)
                turn_keys(n, 3)
                for c in range(2, NC1):
                    dot(n, c, g)

            def outputs(m, g):
                pe.wait_ge(dps_ready if g else dpf_ready, m + 1 - 8 * g)
                last = isinstance(m, int) and m == 15
                pe.wait_ge(kt_moved_act, 8 * m + (8 if last else 16))
                pe.wait_ge(kt_moved_dve, 8 * m + (8 if last else 16))
                for c in range(CH):
                    for t in range(4):
                        mm = pe.transpose(bank[:, c, t * P:t * P + P], d_p[:, 512 * c + t:512 * c + 512:4], ident[:])
                    mm.then_inc(dpt_ready, 1)
                pe.wait_ge(dsc_moved, NC1 * (m + (1 if last else 2)))
                pe.transpose(bank[0:DS, DNEW, P:2 * P], d_p[:, PAST:KEYS], ident[:]).then_inc(dpt_ready, 1)
                if isinstance(m, int) and m == 0:
                    pe.wait_ge(on_done, 2 * NHEAD)
                else:
                    pe.wait_ge(dot_moved, m)
                for c in range(CH):
                    pe.wait_ge(dpt_moved, NC1 * m + c + 1)
                    pe.wait_ge(vd_loaded[c], 16 * (m + 1))
                    for t in range(4):
                        for j in range(NPAIR):
                            mm = pe.matmul(bank[2 * DS * j:2 * DS * j + 2 * DS, MIX, 0:P],
                                           d_pT[:, 4 * c + t, 2 * DS * j:2 * DS * j + 2 * DS], v_ring[:, c, t, j * P:j * P + P],
                                           start=(c == 0 and t == 0), stop=False, skip_group_check=True)
                    mm.then_inc(vd_used, 1)
                pe.wait_ge(vn_loaded, 16 * (m + 1))
                plain_wait(pe, dpt_moved, NC1 * m + NC1)
                for j in range(NPAIR):
                    mm = pe.matmul(bank[2 * DS * j:2 * DS * j + 2 * DS, MIX, 0:P], d_pTn[:, 2 * DS * j:2 * DS * j + 2 * DS],
                                   v_new[:, j * P:j * P + P], start=False, stop=True, skip_group_check=True)
                mm.then_inc(dpv_done, 1)
                pe.wait_ge(od_moved, m + 1)
                pe.transpose(bank[:, MIX, P:2 * P], o_d[:], ident[:]).then_inc(dotr_ready, 1)

            decode_steps(pe, logits, outputs)

        def key_move(eng, n, c, j):
            eng.wait_ge(kt_ready, 16 * n + 4 * c + j + 1)
            if c >= 2:
                eng.wait_ge(dsc_ready, NC1 * n + c - 1)
            elif not (isinstance(n, int) and n == 0):
                eng.wait_ge(dsc_ready, NC1 * n - 2 + c)
            return kT[:, c % 2, j, :], bank[:, j, :]

        def logit_bank(c):
            return bank[:, DSC + c % 2, :] if c < CH else bank[:, DNEW, 0:DS]

        def logit_cols(c):
            return slice(c * 512, c * 512 + 512) if c < CH else slice(PAST, KEYS)

        def is_first(n):
            return isinstance(n, int) and n == 0

        def act_decode(act):
            act.wait_ge(otr_ready, 2 * NHEAD)

            def keys(n, c):
                for j in (0, 2):
                    act.activation(*key_move(act, n, c, j), ACT.Copy).then_inc(kt_moved_act, 1)

            def sigmoids(n, c):
                act.wait_ge(dsc_ready, NC1 * n + c + 1)
                if c == 0:
                    if isinstance(n, int):
                        act.wait_ge(dpf_ready, 8)
                    else:
                        act.wait_ge(dps_ready, n - 8)
                act.activation(d_om[:, logit_cols(c)], logit_bank(c), ACT.Sigmoid, scale=-SCALE).then_inc(dsig_step, 1)
                act.activation(d_s[:, logit_cols(c)], logit_bank(c), ACT.Sigmoid, scale=SCALE).then_inc(dsc_moved, 1)

            def logits(n, g):
                keys(n, 0)
                keys(n, 1)
                if g:
                    sigmoids(n, 0)
                keys(n, 2)
                if g:
                    sigmoids(n, 1)
                keys(n, 3)
                if g:
                    for c in range(2, NC1):
                        sigmoids(n, c)
                else:
                    act.wait_ge(dneg_ready, n + 1)
                    if not is_first(n):
                        act.wait_ge(dinv_done, n)
                        act.wait_ge(dpt_ready, NC1 * n)
                    act.activation(d_p[:], d_s[:], ACT.Exp, bias=d_neg[:, 0:1], scale=SCALE, accum_out=d_sum[:]
                                   ).then_inc(dpf_ready, 1)

            decode_steps(act, logits, lambda m, g: None)

        def dve_decode(dve):
            dve.wait_ge(otr_ready, 2 * NHEAD)
            dve.wait_ge(ct_step, 2)
            dve.tensor_copy(c_hl[0:DB * H], cT8).then_inc(chl_ready, 1)
            dve.wait_ge(chl_ready, 1)
            dve.tensor_tensor(c_hl[DB * H:P], cT8, c_hl[0:DB * H].bitcast(F32), ALU.subtract).then_inc(chl_ready, 1)

            def keys(n, c):
                for j in (1, 3):
                    dve.tensor_copy(*key_move(dve, n, c, j)).then_inc(kt_moved_dve, 1)

            def maxima(n, c):
                if c == 0 and not is_first(n):
                    dve.wait_ge(dpf_ready, n)
                plain_wait(dve, dsc_ready, NC1 * n + c + 1)
                w = 512 if c < CH else DS
                dve.tensor_tensor_reduce(d_s[:, logit_cols(c)], logit_bank(c), zero[:, 0:1].to_broadcast([P, w]),
                                         1.0, LOWEST, ALU.add, ALU.max, d_max[:, c:c + 1]).then_inc(dsc_moved, 1)

            def logits(n, g):
                keys(n, 0)
                keys(n, 1)
                if not g:
                    maxima(n, 0)
                keys(n, 2)
                if not g:
                    maxima(n, 1)
                keys(n, 3)
                if not g:
                    for c in range(2, NC1):
                        maxima(n, c)
                    dve.wait_ge(dsc_moved, NC1 * n + NC1)
                    dve.tensor_reduce(d_max[:, NC1:NC1 + 1], d_max[:, 0:NC1], AX.X, ALU.max).then_inc(dmax_step, 1)
                    dve.wait_ge(dmax_step, n + 1)
                    dve.tensor_scalar(d_neg[:], d_max[:, NC1:NC1 + 1], -SCALE, None, ALU.mult).then_inc(dneg_ready, 1)

            def outputs(m, g):
                if g == 0:
                    dve.wait_ge(dpf_ready, m + 1)
                    if not is_first(m):
                        dve.wait_ge(od_moved, m)
                    dve.reciprocal(d_inv[:], d_sum[:]).then_inc(dinv_done, 1)
                for c in range(NC1):
                    dve.wait_ge(dpt_ready, NC1 * m + c + 1)
                    if c == 0 and not is_first(m):
                        dve.wait_ge(dpv_done, m)
                    if c < CH:
                        dve.tensor_copy(flat(d_pT[:, 4 * c:4 * c + 4, :]), bank[:, c, :]).then_inc(dpt_moved, 1)
                    else:
                        dve.tensor_copy(d_pTn[:], bank[0:DS, DNEW, P:2 * P]).then_inc(dpt_moved, 1)
                n = m + 1
                if not isinstance(n, int) or n < 16:
                    if g == 1 or (isinstance(m, int) and m == 7):
                        scan(n)
                dve.wait_ge(dpv_done, m + 1)
                if not is_first(m):
                    dve.wait_ge(dotr_ready, m)
                if g == 0:
                    dve.wait_ge(dinv_done, m + 1)
                    dve.tensor_scalar(o_d[:], bank[:, MIX, 0:P], d_inv[:, 0:1], None, ALU.mult).then_inc(od_moved, 1)
                else:
                    dve.tensor_copy(o_d[:], bank[:, MIX, 0:P]).then_inc(od_moved, 1)
                dve.wait_ge(dotr_ready, m + 1)
                for hh in range(2):
                    part = slice(hh * HD, hh * HD + HD)
                    src = bank[part, MIX, P:2 * P].rearrange("p (j h s) -> p j h s", j=NPAIR, h=2)[:, :, hh, :]
                    mv = dve.tensor_copy(oT_s[part, g, :, bass.ds((m - 8 * g) * DS, DS)], src)
                mv.then_inc(dot_moved, 1)

            def scan(n):
                dve.wait_ge(dsig_step, NC1 * (n - 7))
                x = d_om[:, ::-1]
                dve.tensor_tensor_scan(x, x, x, 1.0, ALU.mult, ALU.bypass).then_inc(dscan_done, 1)

            decode_steps(dve, logits, outputs)

        def pool_decode(pool):
            pool.wait_ge(otr_ready, 2 * NHEAD)
            pool.wait_ge(sn_moved, 4)

            def current(n, g):
                b = n - 8 * g
                if not is_first(n):
                    pool.wait_ge(dsc_ready, NC1 * n)
                pool.tensor_copy(q_cur[:], qs[:, g, bass.ds(b, 1)].rearrange("p o j m -> p (o j) m")).then_inc(cur_ready, 1)
                pool.tensor_copy(kn_cur[:], kns[:, g, :, bass.ds(b * DS, DS)]).then_inc(cur_ready, 1)
                if g == 0:
                    pool.tensor_copy(pick_cur[:], pickf[:, bass.ds(b, 1)].rearrange("p o m -> p (o m)")).then_inc(cur_ready, 1)

            def product(n):
                pool.wait_ge(dscan_done, n - 7)
                pool.wait_ge(dsc_moved, NC1 * n + NC1)
                pool.wait_ge(dpt_ready, NC1 * n)
                pool.tensor_tensor(d_p[:, 0:KEYS - 1], d_s[:, 0:KEYS - 1], d_om[:, 1:KEYS], ALU.mult).then_inc(dps_ready, 1)

            current(0, 0)
            with pool.Fori(1, 8) as n:
                current(n, 0)
            current(8, 1)
            pool.wait_ge(dpt_ready, NC1 * 8)
            pool.memset(d_p[:, KEYS - 1:KEYS], 0.0).then_inc(dlast_zero, 1)
            pool.wait_ge(dlast_zero, 1)
            product(8)
            with pool.Fori(9, 16) as n:
                current(n, 1)
                product(n)

        gn_loaded, fg_loaded = sem("gn_loaded"), sem("fg_loaded")
        wr_loaded = [sem(f"wr_loaded{c}") for c in range(4)]
        wohi_done, wolo_done = sem("wohi_done"), sem("wolo_done")
        z_loaded, xm_loaded = [sem("z_loaded0"), sem("z_loaded1")], [sem("xm_loaded0"), sem("xm_loaded1")]
        so_ready, so_moved = sem("so_ready"), sem("so_moved")
        msq_done, mms_done, mroot_done = sem("msq_done"), sem("mms_done"), sem("mroot_done")
        sg_done, zg_done, zs_done = sem("sg_done"), sem("zg_done"), sem("zs_done")
        y_ready, ytp_ready, yhi_done, ylo_done = sem("y_ready"), sem("ytp_ready"), sem("yhi_done"), sem("ylo_done")
        m_ready, xo_done, xsq_done, xms_done, xroot_done = (
            sem("m_ready"), sem("xo_done"), sem("xsq_done"), sem("xms_done"), sem("xroot_done"))
        yo_done, y_stored = sem("yo_done"), sem("y_stored")
        OB, SO = 2, 6
        nothing = lambda *a: None

        def row(ap, t):
            return ap[:, bass.ds(t, 1)].rearrange("p o d -> p (o d)")

        def merge_steps(eng, front, gate, back, lag=2):
            def step(t, t2, par):
                static = isinstance(t, int)
                if static and t == 1:
                    gate(2, 0, 2)
                if not static or t < T:
                    front(t, par)
                if not static or (t != 1 and t + 1 < T):
                    gate(t + 1, 1 - par, t2 + 1 + par)
                if not static or t >= lag:
                    back(t - lag, (par + lag) % 2, t2 + (par - lag) // 2 + 1)

            gate(0, 0, 1)
            for t in range(4):
                step(t, t // 2, t % 2)
            with eng.Fori(2, TP // 2) as t2:
                for par in range(2):
                    step(2 * t2 + par, t2, par)
            for t in range(TP, T + lag):
                step(t, t // 2, t % 2)

        def load_wo(sp, chunks):
            for c in chunks:
                sp.dma_start(wo_raw[:, 2 * c:2 * c + 2, :], wo_v[:, 2 * c:2 * c + 2, :]).then_inc(wr_loaded[c], 16)

        def split_wo_hi(act, chunks):
            for c in chunks:
                act.wait_ge(wr_loaded[c], 16)
                if c == 0:
                    act.wait_ge(kt_ready, 16 * 16)
                act.activation(wo_hi[:, 2 * c:2 * c + 2, :], wo_raw[:, 2 * c:2 * c + 2, :], ACT.Copy).then_inc(wohi_done, 1)

        def split_wo_lo(dve, chunks):
            for c in chunks:
                dve.wait_ge(wohi_done, c + 1)
                dve.tensor_tensor(wo_lo[:, 2 * c:2 * c + 2, :], wo_raw[:, 2 * c:2 * c + 2, :],
                                  wo_hi[:, 2 * c:2 * c + 2, :].bitcast(F32), ALU.subtract).then_inc(wolo_done, 1)

        def gate_path(eng, t, par):
            eng.wait_ge(sg_done, t + 1)
            eng.wait_ge(gn_loaded, 32)
            eng.tensor_tensor(zt[:, par], zt[:, par], gn_b[:], ALU.mult).then_inc(zg_done, 1)
            eng.wait_ge(zg_done, t + 1)
            eng.tensor_tensor(zt[:, par], zt[:, par], sg[:], ALU.mult).then_inc(zs_done, 1)

        def sp_merge(sp):
            def load_z(t, par):
                if later(t, 2):
                    sp.wait_ge(y_ready, 2 * (t - 1))
                sp.dma_start(zt[:, par], z_d[bass.ds(t * P, P)]).then_inc(z_loaded[par], 16)

            def load_x(t, par):
                if later(t, 2):
                    sp.wait_ge(xo_done, t - 1)
                src = xs_v if isinstance(t, int) and t == TP else x_prompt[0, bass.ds(t * P, P)]
                sp.dma_start(xt[:, par], src).then_inc(xm_loaded[par], 16)

            def store(t):
                sp.wait_ge(yo_done, t + 1)
                dst = ys_v if isinstance(t, int) and t == TP else y_prompt[0, bass.ds(t * P, P)]
                sp.dma_start(dst, row(o_nat, t)).then_inc(y_stored, 16)

            sp.wait_ge(dsc_ready, NC1 * 16)
            load_z(0, 0)
            sp.wait_ge(dps_ready, 8)
            for g, source in enumerate((out_norm_a, out_norm_b)):
                sp.dma_start(gn_b[:, g * W:g * W + W], source.to_broadcast([P, W])).then_inc(gn_loaded, 16)
            load_wo(sp, (0, 1))
            load_z(1, 1)
            load_wo(sp, (2, 3))
            load_z(2, 0)
            sp.dma_start(fg_b[:], final_norm_g.rearrange("(o d) -> o d", o=1).to_broadcast([P, D])).then_inc(fg_loaded, 16)
            load_x(0, 0)
            load_x(1, 1)

            def step(t, par):
                load_z(t + 1, 1 - par)
                load_x(t, par)
                if later(t, 3):
                    store(t - 3)

            step(2, 0)
            step(3, 1)
            with sp.Fori(2, TP // 2) as t2:
                for par in range(2):
                    step(2 * t2 + par, par)
            load_x(TP, 0)
            for t in range(TP - 3, T):
                store(t)
            sp.wait_ge(y_stored, 16 * T)

        def act_merge(act):
            def gate(t, par, loads):
                if is_first(t):
                    act.wait_ge(dps_ready, 8)
                else:
                    act.wait_ge(msq_done, 2 * t)
                if later(t, 4):
                    act.wait_ge(xsq_done, t - 3)
                if isinstance(t, int) and t == TP:
                    act.wait_ge(so_moved, 2)
                for g in range(2):
                    act.activation(junk[:, g * W:g * W + W], row(o_nat[:, :, g * W:g * W + W], t), ACT.Square,
                                   accum_out=row(m_stat[:, 0, :, g:g + 1], t)).then_inc(msq_done, 1)
                act.wait_ge(z_loaded[par], 16 * loads)
                if not is_first(t):
                    act.wait_ge(zs_done, t)
                act.activation(sg[:], zt[:, par], ACT.Sigmoid).then_inc(sg_done, 1)
                if isinstance(t, int) and t == 1:
                    split_wo_hi(act, (2, 3))

            def front(t, par):
                if is_first(t):
                    split_wo_hi(act, (0, 1))
                for b in range(2):
                    act.wait_ge(ytp_ready, 2 * t + b + 1)
                    if b == 0 and later(t, 2):
                        act.wait_ge(m_ready, 2 * (t - 1))
                    if b == 0 and is_first(t):
                        act.wait_ge(dot_moved, 16)
                    act.activation(yT_hi[:, par, 4 * b:4 * b + 4, :], bank[:, b, :].rearrange("p (k s) -> p k s", k=4),
                                   ACT.Copy).then_inc(yhi_done, 1)

            def back(t, par, loads):
                act.wait_ge(xo_done, t + 1)
                act.wait_ge(msq_done, min(2 * (t + 4), 2 * T) if isinstance(t, int) else 2 * (t + 4))
                if not is_first(t):
                    act.wait_ge(xsq_done, t)
                act.activation(junk[:], row(o_nat, t), ACT.Square, accum_out=row(m_stat[:, 0, :, 2:3], t)
                               ).then_inc(xsq_done, 1)

            merge_steps(act, front, gate, back)

        def dve_merge(dve):
            def gate(t, par, loads):
                if isinstance(t, int) and t == 1:
                    for g in range(2):
                        dve.wait_ge(so_ready, g + 1)
                        dve.tensor_copy(o_nat[:, TP, g * W:g * W + W], bank[:, SO + g, :]).then_inc(so_moved, 1)
                dve.wait_ge(msq_done, 2 * t + 2)
                dve.tensor_scalar(row(m_stat[:, 1, :, 0:2], t), row(m_stat[:, 0, :, 0:2], t), 1.0 / W, EPS, ALU.mult, ALU.add
                                  ).then_inc(mms_done, 1)
                if is_first(t):
                    gate_path(dve, t, par)
                if isinstance(t, int) and t == 1:
                    split_wo_lo(dve, (2, 3))

            def front(t, par):
                dve.wait_ge(mroot_done, t + 1)
                dve.wait_ge(zs_done, t + 1)
                if is_first(t):
                    dve.wait_ge(dpt_ready, NC1 * 16)
                else:
                    dve.wait_ge(ytp_ready, 2 * t)
                for g in range(2):
                    dve.scalar_tensor_tensor(out=yg[:, g * W:g * W + W], in0=row(o_nat[:, :, g * W:g * W + W], t),
                                             scalar=row(m_stat[:, 2, :, g:g + 1], t), in1=zt[:, par, g * W:g * W + W],
                                             op0=ALU.mult, op1=ALU.mult).then_inc(y_ready, 1)
                if is_first(t):
                    split_wo_lo(dve, (0, 1))
                for b in range(2):
                    dve.wait_ge(yhi_done, 2 * t + b + 1)
                    dve.tensor_tensor(yT_lo[:, par, 4 * b:4 * b + 4, :], bank[:, b, :].rearrange("p (k s) -> p k s", k=4),
                                      yT_hi[:, par, 4 * b:4 * b + 4, :].bitcast(F32), ALU.subtract).then_inc(ylo_done, 1)

            def finish(t):
                dve.wait_ge(xroot_done, t + 1)
                dve.scalar_tensor_tensor(out=row(o_nat, t), in0=row(o_nat, t), scalar=row(m_stat[:, 2, :, 2:3], t),
                                         in1=fg_b[:], op0=ALU.mult, op1=ALU.mult).then_inc(yo_done, 1)

            def back(t, par, loads):
                if is_first(t):
                    dve.wait_ge(fg_loaded, 16)
                dve.wait_ge(m_ready, 2 * t + 2)
                dve.wait_ge(xm_loaded[par], 16 * loads)
                dve.tensor_tensor(row(o_nat, t), flat(bank[:, OB + 2 * par:OB + 2 * par + 2, :]), xt[:, par], ALU.add
                                  ).then_inc(xo_done, 1)
                if later(t, 1):
                    finish(t - 1)
                dve.wait_ge(xsq_done, t + 1)
                dve.tensor_scalar(row(m_stat[:, 1, :, 2:3], t), row(m_stat[:, 0, :, 2:3], t), 1.0 / D, EPS, ALU.mult, ALU.add
                                  ).then_inc(xms_done, 1)

            merge_steps(dve, front, gate, back)
            finish(TP)

        def pool_merge(pool):
            def gate(t, par, loads):
                if not is_first(t):
                    gate_path(pool, t, par)
                pool.wait_ge(mms_done, t + 1)
                pool.tensor_tensor(row(m_stat[:, 2, :, 0:2], t), row(m_stat[:, 1, :, 0:2], t), neghalf[:, 0:2], ALU.pow
                                   ).then_inc(mroot_done, 1)

            def back(t, par, loads):
                pool.wait_ge(xms_done, t + 1)
                pool.tensor_tensor(row(m_stat[:, 2, :, 2:3], t), row(m_stat[:, 1, :, 2:3], t), neghalf[:, 0:1], ALU.pow
                                   ).then_inc(xroot_done, 1)

            merge_steps(pool, nothing, gate, back)

        def pe_merge(pe):
            def front(t, par):
                if isinstance(t, int) and t == 1:
                    multiply(0, 0)
                pe.wait_ge(y_ready, 2 * t + 2)
                if is_first(t):
                    pe.wait_ge(dpt_moved, NC1 * 16)
                else:
                    pe.wait_ge(ylo_done, 2 * t)
                for b in range(2):
                    for k in range(4):
                        mm = pe.transpose(bank[:, b, k * P:k * P + P], yg[:, (4 * b + k) * P:(4 * b + k) * P + P], ident[:])
                    mm.then_inc(ytp_ready, 1)
                if is_first(t):
                    pe.wait_ge(dot_moved, 16)
                    for g in range(2):
                        for j in range(NPAIR):
                            mm = pe.transpose(bank[:, SO + g, j * P:j * P + P], oT_s[:, g, j, :], ident[:])
                        mm.then_inc(so_ready, 1)

            def products(t, par, loads):
                if not is_first(t):
                    multiply(t, par)

            def multiply(t, par):
                pe.wait_ge(ylo_done, 2 * t + 2)
                if later(t, 2):
                    pe.wait_ge(xo_done, t - 1)
                for part in range(2):
                    cols = slice(part * W, part * W + W)
                    for k in range(KD):
                        if is_first(t) and part == 0 and k % 2 == 0:
                            pe.wait_ge(wolo_done, k // 2 + 1)
                        for n, (a, b) in enumerate(((yT_hi, wo_hi), (yT_hi, wo_lo), (yT_lo, wo_hi))):
                            mm = pe.matmul(bank[:, OB + 2 * par + part, :], a[:, par, k, :], b[:, k, cols],
                                           start=(k == 0 and n == 0), stop=(k == KD - 1 and n == 2))
                    mm.then_inc(m_ready, 1)

            merge_steps(pe, front, nothing, products, lag=1)

        block_ = keep.enter_context(nc.Block())

        @block_.gpsimd
        def _(pool):
            pool.memset(ident[:], 0.0).then_inc(pool_step, 1)
            pool.memset(neghalf[:], -0.5).then_inc(pool_step, 1)
            pool.wait_ge(pool_step, 2)
            pool.affine_select(out=ident[:], in_=ident[:], compare_op=ALU.not_equal, fill=1.0, base=0,
                               pattern=[[-1, P]], channel_multiplier=1).then_inc(consts, 1)
            pool.memset(identb[:], 0.0).then_inc(pool_step, 1)
            pool.memset(mask[0][:], 0.0).then_inc(pool_step, 1)
            pool.memset(mask[1][:], 0.0).then_inc(pool_step, 1)
            pool.memset(tselb[:], 0.0).then_inc(pool_step, 1)
            pool.memset(zero[:], 0.0).then_inc(pool_step, 1)
            pool.memset(pickf[:], 0.0).then_inc(pool_step, 1)
            pool.wait_ge(pool_step, 8)
            pool.affine_select(out=identb[:], in_=identb[:], compare_op=ALU.not_equal, fill=1.0, base=0,
                               pattern=[[-1, P]], channel_multiplier=1).then_inc(consts, 1)
            for g in range(2):
                pool.affine_select(out=mask[g][:], in_=mask[g][:], compare_op=ALU.is_ge, fill=MASKED, base=-g,
                                   pattern=[[-1, P]], channel_multiplier=1).then_inc(consts, 1)
            pool.affine_select(out=tselb[:].rearrange("p (h t) -> p h t", h=H), in_=tselb[:].rearrange("p (h t) -> p h t", h=H),
                               compare_op=ALU.not_equal, fill=1.0, base=0, pattern=[[0, H], [-1, DS]],
                               channel_multiplier=1).then_inc(consts, 1)
            pick = pickf[:].rearrange("p b (h t) -> p b h t", h=H)
            for half in range(2):
                pool.affine_select(out=pick, in_=pick, compare_op=ALU.not_equal, fill=1.0, base=-DB * H * half,
                                   pattern=[[-H, DB], [-1, H], [0, DS]], channel_multiplier=1).then_inc(consts, 1)
                pool.wait_ge(consts, 6 + half)
            pool_project(pool)
            pool.memset(qs[:], 0.0).then_inc(qs_zero, 1)
            pool_prompt(pool)
            pool_decode(pool)
            pool_merge(pool)

        @block_.sync
        def _(sp):
            sp_project(sp)
            sp_prompt(sp)
            sp_decode(sp)
            sp_merge(sp)

        @block_.scalar
        def _(act):
            act_project(act)
            act_prompt(act)
            act_decode(act)
            act_merge(act)

        @block_.vector
        def _(dve):
            dve_project(dve)
            dve_prompt(dve)
            dve_decode(dve)
            dve_merge(dve)

        @block_.tensor
        def _(pe):
            pe_project(pe)
            pe_prompt(pe)
            pe_decode(pe)
            pe_merge(pe)


_INS = ["x_prompt", "x_sample", "cache_fox_k", "cache_fox_v", "cache_fox_logf", "cache_sb_k", "cache_sb_v",
        "norm_g", "w_in", "b_f", "out_norm_a", "out_norm_b", "w_out", "final_norm_g"]


def kernel(**inputs):
    import numpy as np
    import concourse.bacc as bacc
    from concourse.bass_utils import run_bass_kernel_spmd

    nc = bacc.Bacc("TRN2", target_bir_lowering=False, num_devices=1)
    arrays, args = {}, []
    for name in _INS:
        a = np.ascontiguousarray(inputs[name])
        arrays[f"in_{name}"] = a
        args.append(nc.dram_tensor(f"in_{name}", a.shape, mybir.dt.from_np(a.dtype), kind="ExternalInput").ap())
    xp, xs, kc = (inputs[n].shape for n in ("x_prompt", "x_sample", "cache_fox_k"))
    heads, hd = kc[3], kc[4]
    prompt, sample = (1, xp[0], xp[1], heads), (1, xs[0], xs[1], heads)
    shapes = [xp, xs] + [s for lead in (prompt, sample) for s in (lead + (hd,), lead + (hd,), lead, lead + (hd,), lead + (hd,))]
    for i, shape in enumerate(shapes):
        args.append(nc.dram_tensor(f"out_{i}", shape, F32, kind="ExternalOutput").ap())
    build(nc, *args)
    r = run_bass_kernel_spmd(nc, [arrays], core_ids=[0])
    return tuple(r.results[0][f"out_{i}"] for i in range(len(shapes)))
```
